# Optimizing a Trainium2 kernel written in Bass

```python
import math
import jax, jax.numpy as jnp
from jax import lax
import numpy as np

D_MODEL = 1024
BATCH = 1
SEQ = 1024
DEPTH = 1
DEC_BATCH = 8
DEC_SEQ = 4
PAST_LEN = 8192
PAGE_SIZE = 128

MIX_WIDTH = (3 * D_MODEL) // 2
GROUP_WIDTH = MIX_WIDTH // 3
RET_HEADS = 4
RET_DK = GROUP_WIDTH // RET_HEADS
RET_DV = GROUP_WIDTH // RET_HEADS
RET_CHUNK = 128
LRU_WIDTH = GROUP_WIDTH
LRU_BLOCKS = 8
LRU_BLOCK_W = LRU_WIDTH // LRU_BLOCKS
LRU_C = 8.0
CONV_W = 4
SWA_HEADS = 4
SWA_KV_HEADS = 2
SWA_GROUP = SWA_HEADS // SWA_KV_HEADS
SWA_HEAD_DIM = GROUP_WIDTH // SWA_HEADS
WINDOW = 128
NORM_EPS = 1e-6
NEG_INF = -1e30

SPLIT_SIZES = (RET_HEADS * RET_DK, RET_HEADS * RET_DK, RET_HEADS * RET_DV, RET_HEADS * RET_DV,
               LRU_WIDTH, LRU_WIDTH,
               SWA_HEADS * SWA_HEAD_DIM, SWA_KV_HEADS * SWA_HEAD_DIM, SWA_KV_HEADS * SWA_HEAD_DIM,
               SWA_HEADS * SWA_HEAD_DIM)
IN_WIDTH = sum(SPLIT_SIZES)
SPLIT_IDX = tuple(sum(SPLIT_SIZES[:i + 1]) for i in range(len(SPLIT_SIZES) - 1))

kernel_name = 'hymba_retention_rglru_swasink_step'

def _rmsnorm(x, g):
    x32 = x.astype(jnp.float32)
    y = x32 * lax.rsqrt(jnp.mean(x32 * x32, axis=-1, keepdims=True) + NORM_EPS)
    return (y * g.astype(jnp.float32)).astype(x.dtype)

def _retention(q, k, v, s0):
    B, T, H, DK = q.shape
    DV = v.shape[-1]
    C = math.gcd(T, RET_CHUNK)
    n = T // C
    f32 = jnp.float32
    log_g = jnp.log1p(-jnp.power(2.0, -5.0 - jnp.arange(H, dtype=f32)))
    qc = q.astype(f32).reshape(B, n, C, H, DK)
    kc = (k.astype(f32) * (DK ** -0.5)).reshape(B, n, C, H, DK)
    vc = v.astype(f32).reshape(B, n, C, H, DV)
    idx = jnp.arange(C, dtype=f32)
    diff = idx[:, None] - idx[None, :]
    causal = diff >= 0
    decay_mask = jnp.where(causal[None], jnp.exp(jnp.where(causal, diff, 0.0)[None] * log_g[:, None, None]), 0.0)
    scores = jnp.einsum('bnihd,bnjhd->bnhij', qc, kc) * decay_mask[None, None]
    intra = jnp.einsum('bnhij,bnjhe->bnihe', scores, vc)
    k_dec = kc * jnp.exp((C - 1 - idx)[:, None] * log_g[None, :])[None, None, :, :, None]
    kv = jnp.einsum('bnjhd,bnjhe->nbhde', k_dec, vc)
    chunk_decay = jnp.exp(C * log_g)[None, :, None, None]

    def step(S, kv_c):
        return chunk_decay * S + kv_c, S

    s_final, s_prev = lax.scan(step, s0.astype(f32), kv)
    q_dec = qc * jnp.exp((idx + 1.0)[:, None] * log_g[None, :])[None, None, :, :, None]
    cross = jnp.einsum('bnihd,nbhde->bnihe', q_dec, s_prev)
    o = (intra + cross).reshape(B, T, H, DV)
    return o.astype(q.dtype), s_final.astype(s0.dtype)

def _lin_combine(left, right):
    a1, b1 = left
    a2, b2 = right
    return a1 * a2, a2 * b1 + b2

def _rglru(xb, conv_buf, h0, pos0, conv_w, conv_b, w_r, b_r, w_i, b_i, lam):
    B, T, W = xb.shape
    f32 = jnp.float32
    xc = jnp.concatenate([conv_buf.astype(xb.dtype), xb], axis=1)
    conv = conv_b.astype(f32)[None, None, :]
    for j in range(CONV_W):
        conv = conv + conv_w[j].astype(f32) * xc[:, j:j + T].astype(f32)
    new_buf = xc[:, T:]
    xg = conv.reshape(B, T, LRU_BLOCKS, LRU_BLOCK_W)
    r = jax.nn.sigmoid(jnp.einsum('btnd,nde->btne', xg, w_r.astype(f32)).reshape(B, T, W) + b_r.astype(f32))
    i = jax.nn.sigmoid(jnp.einsum('btnd,nde->btne', xg, w_i.astype(f32)).reshape(B, T, W) + b_i.astype(f32))
    log_a = -LRU_C * r * jax.nn.softplus(-lam.astype(f32))
    a = jnp.exp(log_a)
    pos = pos0 + jnp.arange(T)
    mult = jnp.where((pos == 0)[None, :, None], 1.0, jnp.sqrt(-jnp.expm1(2.0 * log_a)))
    u = mult * i * conv
    u = u.at[:, 0].add(a[:, 0] * h0.astype(f32))
    _, h = lax.associative_scan(_lin_combine, (a, u), axis=1)
    return h.astype(xb.dtype), h[:, -1].astype(h0.dtype), new_buf.astype(conv_buf.dtype)

def _alibi_slopes():
    return jnp.power(2.0, -8.0 * jnp.arange(1, SWA_HEADS + 1, dtype=jnp.float32) / SWA_HEADS)

def _swa_core(q, k, v, q_pos, k_pos, sinks):
    f32 = jnp.float32
    s = jnp.einsum('bnqhgd,bnkhd->bnhgqk', q.astype(f32), k.astype(f32)) * (SWA_HEAD_DIM ** -0.5)
    dist = q_pos[:, :, None] - k_pos[:, None, :]
    valid = (dist >= 0) & (dist < WINDOW) & (k_pos[:, None, :] >= 0)
    slopes = _alibi_slopes().reshape(SWA_KV_HEADS, SWA_GROUP)
    s = s - slopes[None, None, :, :, None, None] * dist.astype(f32)[None, :, None, None]
    s = jnp.where(valid[None, :, None, None], s, NEG_INF)
    sink = sinks.astype(f32).reshape(SWA_KV_HEADS, SWA_GROUP)[None, None, :, :, None, None]
    m = jnp.maximum(jnp.max(s, axis=-1, keepdims=True), sink)
    p = jnp.exp(s - m)
    denom = jnp.sum(p, axis=-1, keepdims=True) + jnp.exp(sink - m)
    return jnp.einsum('bnhgqk,bnkhd->bnqhgd', p / denom, v.astype(f32))

def _swa_prompt(q, k, v, sinks):
    B, T = q.shape[:2]
    nb = T // WINDOW
    qb = q.reshape(B, nb, WINDOW, SWA_KV_HEADS, SWA_GROUP, SWA_HEAD_DIM)
    kb = k.reshape(B, nb, WINDOW, SWA_KV_HEADS, SWA_HEAD_DIM)
    vb = v.reshape(B, nb, WINDOW, SWA_KV_HEADS, SWA_HEAD_DIM)
    k_band = jnp.concatenate([jnp.concatenate([jnp.zeros_like(kb[:, :1]), kb[:, :-1]], axis=1), kb], axis=2)
    v_band = jnp.concatenate([jnp.concatenate([jnp.zeros_like(vb[:, :1]), vb[:, :-1]], axis=1), vb], axis=2)
    pos = jnp.arange(T, dtype=jnp.int32).reshape(nb, WINDOW)
    k_pos = jnp.concatenate([pos - WINDOW, pos], axis=1)
    o = _swa_core(qb, k_band, v_band, pos, k_pos, sinks)
    return o.reshape(B, T, SWA_HEADS * SWA_HEAD_DIM).astype(q.dtype), k[:, T - WINDOW:], v[:, T - WINDOW:]

def _swa_sample(q, k, v, kbuf, vbuf, pos0, sinks):
    B, T = q.shape[:2]
    k_all = jnp.concatenate([kbuf.astype(k.dtype), k], axis=1)
    v_all = jnp.concatenate([vbuf.astype(v.dtype), v], axis=1)
    q_pos = (pos0 + jnp.arange(T, dtype=jnp.int32))[None]
    k_pos = (pos0 - WINDOW + jnp.arange(WINDOW + T, dtype=jnp.int32))[None]
    qb = q.reshape(B, 1, T, SWA_KV_HEADS, SWA_GROUP, SWA_HEAD_DIM)
    o = _swa_core(qb, k_all[:, None], v_all[:, None], q_pos, k_pos, sinks)
    new_k = k_all[:, T:].astype(kbuf.dtype)
    new_v = v_all[:, T:].astype(vbuf.dtype)
    return o.reshape(B, T, SWA_HEADS * SWA_HEAD_DIM).astype(q.dtype), new_k, new_v

def _layer(x, pos0, s0, h0, conv_buf, kbuf, vbuf, norm_g, w_in, w_out, ret_g, conv_w, conv_b,
           w_r, b_r, w_i, b_i, lam, q_g, k_g, sinks):
    B, T, _ = x.shape
    h = _rmsnorm(x, norm_g)
    proj = jnp.einsum('btd,de->bte', h, w_in)
    qa, ka, va, ga, xb, gb, qc, kc, vc, gc = jnp.split(proj, SPLIT_IDX, axis=-1)
    oa, s_new = _retention(qa.reshape(B, T, RET_HEADS, RET_DK), ka.reshape(B, T, RET_HEADS, RET_DK),
                           va.reshape(B, T, RET_HEADS, RET_DV), s0)
    oa = _rmsnorm(oa, ret_g.reshape(RET_HEADS, RET_DV)).reshape(B, T, RET_HEADS * RET_DV)
    ob, h_new, conv_new = _rglru(xb, conv_buf, h0, pos0, conv_w, conv_b, w_r, b_r, w_i, b_i, lam)
    qc = _rmsnorm(qc.reshape(B, T, SWA_HEADS, SWA_HEAD_DIM), q_g)
    kc = _rmsnorm(kc.reshape(B, T, SWA_KV_HEADS, SWA_HEAD_DIM), k_g)
    vc = vc.reshape(B, T, SWA_KV_HEADS, SWA_HEAD_DIM)
    if kbuf is None:
        oc, k_new, v_new = _swa_prompt(qc, kc, vc, sinks)
    else:
        oc, k_new, v_new = _swa_sample(qc, kc, vc, kbuf, vbuf, pos0, sinks)
    mixed = jnp.concatenate([oa * jax.nn.silu(ga), ob * jax.nn.silu(gb), oc * jax.nn.silu(gc)], axis=-1)
    y = x + jnp.einsum('bte,ed->btd', mixed, w_out)
    return y, s_new, h_new, conv_new, k_new, v_new

def setup_inputs(seed: int = 0) -> dict:
    key = jax.random.key(seed)
    ks = jax.random.split(key, 24)
    f32 = jnp.float32
    nrm = lambda k, shape: jax.random.normal(k, shape, dtype=f32)
    u = jax.random.uniform(ks[19], (DEPTH, LRU_WIDTH), dtype=f32, minval=0.9, maxval=0.999)
    p = jnp.power(u, 1.0 / LRU_C)
    lru_lambda = jnp.log(p) - jnp.log1p(-p)
    return {
        'x_prompt': nrm(ks[0], (BATCH, SEQ, D_MODEL)),
        'x_sample': nrm(ks[1], (DEC_BATCH, DEC_SEQ, D_MODEL)),
        'state_ret': 0.5 * nrm(ks[2], (DEPTH, DEC_BATCH, RET_HEADS, RET_DK, RET_DV)),
        'state_lru': 0.5 * nrm(ks[3], (DEPTH, DEC_BATCH, LRU_WIDTH)),
        'state_conv': nrm(ks[4], (DEPTH, DEC_BATCH, CONV_W - 1, LRU_WIDTH)),
        'cache_swa_k': nrm(ks[5], (DEPTH, DEC_BATCH, WINDOW, SWA_KV_HEADS, SWA_HEAD_DIM)),
        'cache_swa_v': nrm(ks[6], (DEPTH, DEC_BATCH, WINDOW, SWA_KV_HEADS, SWA_HEAD_DIM)),
        'norm_g': 1.0 + 0.02 * nrm(ks[7], (DEPTH, D_MODEL)),
        'w_in': nrm(ks[8], (DEPTH, D_MODEL, IN_WIDTH)) * D_MODEL ** -0.5,
        'w_out': nrm(ks[9], (DEPTH, MIX_WIDTH, D_MODEL)) * MIX_WIDTH ** -0.5,
        'ret_norm_g': 1.0 + 0.02 * nrm(ks[10], (DEPTH, RET_HEADS * RET_DV)),
        'conv_w': nrm(ks[11], (DEPTH, CONV_W, LRU_WIDTH)) * CONV_W ** -0.5,
        'conv_b': 0.02 * nrm(ks[12], (DEPTH, LRU_WIDTH)),
        'w_rgate': nrm(ks[13], (DEPTH, LRU_BLOCKS, LRU_BLOCK_W, LRU_BLOCK_W)) * LRU_BLOCK_W ** -0.5,
        'b_rgate': 0.02 * nrm(ks[14], (DEPTH, LRU_WIDTH)),
        'w_igate': nrm(ks[15], (DEPTH, LRU_BLOCKS, LRU_BLOCK_W, LRU_BLOCK_W)) * LRU_BLOCK_W ** -0.5,
        'b_igate': 0.02 * nrm(ks[16], (DEPTH, LRU_WIDTH)),
        'lru_lambda': lru_lambda,
        'q_norm_g': 1.0 + 0.02 * nrm(ks[17], (DEPTH, SWA_HEAD_DIM)),
        'k_norm_g': 1.0 + 0.02 * nrm(ks[18], (DEPTH, SWA_HEAD_DIM)),
        'attn_sinks': nrm(ks[20], (DEPTH, SWA_HEADS)),
    }

def reference(x_prompt, x_sample, state_ret, state_lru, state_conv, cache_swa_k, cache_swa_v,
              norm_g, w_in, w_out, ret_norm_g, conv_w, conv_b, w_rgate, b_rgate, w_igate, b_igate,
              lru_lambda, q_norm_g, k_norm_g, attn_sinks):
    yp, ys = x_prompt, x_sample
    Bp = x_prompt.shape[0]
    dt = x_prompt.dtype
    p_ret, p_lru, p_conv, p_k, p_v = [], [], [], [], []
    s_ret, s_lru, s_conv, s_k, s_v = [], [], [], [], []
    for l in range(DEPTH):
        wts = (norm_g[l], w_in[l], w_out[l], ret_norm_g[l], conv_w[l], conv_b[l],
               w_rgate[l], b_rgate[l], w_igate[l], b_igate[l], lru_lambda[l],
               q_norm_g[l], k_norm_g[l], attn_sinks[l])
        yp, a1, a2, a3, a4, a5 = _layer(
            yp, 0,
            jnp.zeros((Bp, RET_HEADS, RET_DK, RET_DV), dt),
            jnp.zeros((Bp, LRU_WIDTH), dt),
            jnp.zeros((Bp, CONV_W - 1, LRU_WIDTH), dt),
            None, None, *wts)
        p_ret.append(a1); p_lru.append(a2); p_conv.append(a3); p_k.append(a4); p_v.append(a5)
        ys, b1, b2, b3, b4, b5 = _layer(
            ys, PAST_LEN, state_ret[l], state_lru[l], state_conv[l], cache_swa_k[l], cache_swa_v[l], *wts)
        s_ret.append(b1); s_lru.append(b2); s_conv.append(b3); s_k.append(b4); s_v.append(b5)
    return (yp, ys,
            jnp.stack(p_ret), jnp.stack(p_lru), jnp.stack(p_conv), jnp.stack(p_k), jnp.stack(p_v),
            jnp.stack(s_ret), jnp.stack(s_lru), jnp.stack(s_conv), jnp.stack(s_k), jnp.stack(s_v))


_drawn_inputs = setup_inputs


def setup_inputs(seed=0):
    import zlib

    import numpy as np

    out = dict(_drawn_inputs(seed))
    spreads = {}
    factors = {'ret_norm_g': 23.288,
     'b_rgate': 8.0,
     'b_igate': 7.087,
     'q_norm_g': 49.637,
     'k_norm_g': 9.03,
     'attn_sinks': 64.0}
    for name, (base, spread) in spreads.items():
        noise = np.random.default_rng([zlib.crc32(name.encode()), seed]).standard_normal(out[name].shape)
        drawn = base * np.exp(spread * noise) if base else spread * noise
        out[name] = __import__('jax').numpy.asarray(drawn.astype(out[name].dtype))
    for name, factor in factors.items():
        out[name] = (out[name] * factor).astype(out[name].dtype)
    return out
```

```python
from contextlib import ExitStack

import numpy as np

import concourse.bass as bass
from concourse import mybir

F32 = mybir.dt.float32
F32R = mybir.dt.float32r
ALU = mybir.AluOpType
ACT = mybir.ActivationFunctionType
AX = mybir.AxisListType

P = 128
D = 1024
SEQ = 1024
DB, DS = 8, 4
NS = DB * DS
TOK = SEQ + NS
NT = SEQ // P
KD = D // P
GW = 512
H = 4
DH = GW // H
KM = 3 * GW // P
W_IN = 9 * GW
UNIT = 256
NU = W_IN // UNIT
CH = TOK // 3
CONV = 4
WINDOW = 128
EPS = 1e-6
NEG = -1e30
SCALE = DH ** -0.5
LRU_C = 8.0
AKEYS = WINDOW + NS

UNITS = [("v", 0), ("qk", 0), ("v", 1), ("qk", 1), ("qk", 2), ("qk", 3), ("gB", 0), ("gB", 1),
         ("xb", 0), ("xb", 1), ("gC", 0), ("gC", 1), ("kvC", 0), ("qC", 0), ("kvC", 1), ("qC", 1),
         ("gA", 0), ("gA", 1)]
TOKEN_MAJOR = ("v", "kvC", "qC")


def n_groups(u):
    return NT + 1 if UNITS[u][0] in TOKEN_MAJOR else 6


FIRST_GROUP = [sum(n_groups(v) for v in range(u)) for u in range(NU + 1)]
GROUPS = [(u, j) for u in range(NU) for j in range(n_groups(u))]


def freed(u, j):
    kind, i = UNITS[u]
    if kind in ("kvC", "qC"):
        return "kn_set" if kind == "kvC" else "qn_set", 9 * i + j + 1
    return "act_freed", sum(UNITS[v][0] not in ("kvC", "qC") for v, _ in GROUPS[:FIRST_GROUP[u] + j + 1])


PAR = {"ret_g": 0, "conv_w": 4, "conv_b": 20, "b_r": 24, "b_i": 28, "lam": 32, "sink": 36, "sink_s": 40}
N_PAR = 42
C_MASK, C_QDEC, C_KDEC, C_MASKS, C_QDECS, C_VSEL = 0, 512, 1024, 1028, 1156, 1284
N_CR = 1316
C_BIAS, C_BIASS = 0, 1024
N_CC = C_BIASS + 2 * AKEYS


def layer(nc, io):
    gammas = [float(1.0 - 2.0 ** (-5.0 - h)) for h in range(H)]
    with ExitStack() as ctx:
        def sb(name, shape, dt=F32, scope=ctx):
            return scope.enter_context(nc.sbuf_tensor(name, shape, dt))

        def sem(name):
            return ctx.enter_context(nc.semaphore(name))

        big = sb("big", [P, 25088], F32R)
        h_hi = big[:, 0:KD * TOK].rearrange("p (k n) -> p k n", k=KD)
        h_lo = big[:, KD * TOK:2 * KD * TOK].rearrange("p (k n) -> p k n", k=KD)
        w_base = 2 * KD * TOK
        wsz = KD * UNIT

        def w_part(slot, part):
            a = w_base + (2 * slot + part) * wsz
            return big[:, a:a + wsz]

        wo_hi = big[:, 0:KM * D].rearrange("p (k n) -> p k n", k=KM)
        wo_lo = big[:, KM * D:2 * KM * D].rearrange("p (k n) -> p k n", k=KM)
        mixed = sb("mixed", [P, 3 * H, TOK])
        raw = sb("raw", [P, wsz])
        ident = sb("ident", [P, P])
        ones = sb("ones", [P, P])
        par = sb("par", [P, N_PAR])
        gain = sb("gain", [P, 2, DH])
        st_T = sb("st_T", [P, H, NS])
        tails = sb("tails", [P, H, 36])
        tail_rows = sb("tail_rows", [36, GW])
        stat = sb("stat", [P, 64])
        neghalf = sb("neghalf", [P, NS])
        junk = sb("junk", [P, UNIT])
        sp_t = sb("sp_t", [P, 8, H])

        flat = mixed[:, 0:H, :].rearrange("p a n -> p (a n)")
        x_in = [flat[:, i * D:(i + 1) * D] for i in range(2)]
        g_row = flat[:, 2 * D:3 * D]
        x_sq = flat[:, 3 * D:4 * D]
        qk = [mixed[:, 2 * H + 2 * (h % 2):2 * H + 2 * (h % 2) + 2, :] for h in range(H)]

        with ExitStack() as r:
            v_tok = sb("v_tok", [P, 2, NT + 1, UNIT], scope=r)
            cr = sb("cr", [P, N_CR], scope=r)
            s0 = sb("s0", [P, DB, DH], scope=r)
            v_sel = sb("v_sel", [NS, DB, DH], scope=r)
            sT = sb("sT", [P, 2, P], scope=r)
            k_dec = sb("k_dec", [P, 2, P], scope=r)
            q_dec = sb("q_dec", [P, 2, P], scope=r)
            o_nrm = sb("o_nrm", [P, 2, P], scope=r)
            S = sb("S", [P, 2, P], scope=r)
            o_sq = sb("o_sq", [P, P], scope=r)
            o_rs = sb("o_rs", [P, 2, NS], scope=r)
            st_rows = sb("st_rows", [NS, GW], scope=r)
        with ExitStack() as r:
            XW = 3 + SEQ + DB * 7
            xb = sb("xb", [P, 2, XW], scope=r)
            cv = sb("cv", [P, 2, TOK], scope=r)
            rg = sb("rg", [P, TOK], scope=r)
            ig = sb("ig", [P, TOK], scope=r)
            aa = sb("aa", [P, TOK], scope=r)
            tt = sb("tt", [P, TOK], scope=r)
            wg = sb("wg", [P, 2, H, P], scope=r)
        with ExitStack() as r:
            kT = sb("kT", [P, 2, TOK], scope=r)
            v_c = sb("v_c", [P, 2, NT + 1, DH], scope=r)
            cc = sb("cc", [P, N_CC], scope=r)
            qn = sb("qn", [P, 2, 2 * DH], scope=r)
            kn = sb("kn", [P, 2, DH], scope=r)
            qT = sb("qT", [P, 2, 2 * P], scope=r)
            pr = sb("pr", [P, 2, 2, 2 * P], scope=r)
            pT = sb("pT", [P, 2, 4 * P], scope=r)
            cache = sb("cache", [P, DB, DH], scope=r)
            kcT = sb("kcT", [P, DB, P], scope=r)
        gate_tmp = kT[:, 0, 0:2 * CH].rearrange("p (a n) -> p a n", a=2)
        with ExitStack() as r:
            m_hi = sb("m_hi", [P, 2, KM, P], F32R, scope=r)
            m_lo = sb("m_lo", [P, 2, KM, P], F32R, scope=r)
            x_res = sb("x_res", [P, 2, D], scope=r)
            y_out = sb("y_out", [P, 2, D], scope=r)

        pb = [ctx.enter_context(nc.psum_tensor(f"proj{i}", [P, 512], F32)) for i in range(3)]
        bb = [ctx.enter_context(nc.psum_tensor(f"branch{i}", [P, 512], F32)) for i in range(5)]

        names = """norm_in const_in cr_in wg_in cc_in x_tile0 x_tile1 raw_in s0_in kcache_in vcache_in
            x_again0 x_again1 wo_in0 wo_in1
            stored_cache stored_ret stored_tails stored_kv stored_y0 stored_y1
            ones_set x_ss x_pow x_scaled x_turned_a x_turned_b h_hi_set h_lo_set
            w_hi_set w_lo_set proj_done act_freed
            scores_done kturn_done masked kdec_set qdec_set vsel_set o_done kv_done kv2_done s_set s2_set
            o_ss o_pow o_ms o_set oT_done mix_a
            st_turned st_copied lam_exp decay_set conv_set gates_done gates_read exp_set m2_set m_set
            lru_set xb_set tails_turned tails_copied
            k_ss k_pow kn_set kT_done kT_set q_ss q_pow qn_half qn_set qT_done qT_set
            sc_done biased mx_set ex_set pr_set pT_done pT_set av_done mix_c
            kc_turned kc_copied ssT_done ssT_part ssT_set ss_done smx_set sex_set spr_set spT_done
            spT_part spT_set sav_done smix_half smix_c
            mix_g m_hi_set m_lo_set y_done y_set
            chain_v chain_a chain_p""".split()
        S_ = {n: sem(n) for n in names}

        def stat_col(i, n=1):
            return stat[:, i:i + n]

        block = ctx.enter_context(nc.Block())

        def tile_rows(t):
            return P if t < NT else NS

        def chunk_cols(c):
            return slice(c * P, c * P + tile_rows(c))

        n_stores = {}

        @block.sync
        def _(sp):
            def store(dst, src, name):
                sp.dma_start(dst, src).then_inc(S_[name], 16)
                n_stores[name] = n_stores.get(name, 0) + 16

            def load_w(u):
                if u > 0:
                    sp.wait_ge(S_["w_hi_set"], u)
                    sp.wait_ge(S_["w_lo_set"], u)
                sp.dma_start(raw[:], io["w_units"][u]).then_inc(S_["raw_in"], 16)

            def x_rows(t):
                return io["x_prompt"][t * P:(t + 1) * P, :] if t < NT else io["x_sample"]

            sp.dma_start(x_in[0], x_rows(0)).then_inc(S_["x_tile0"], 16)
            load_w(0)
            sp.dma_start(g_row, io["norm_g"].partition_broadcast(P)).then_inc(S_["norm_in"], 16)
            sp.dma_start(ident[:], io["c_ident"]).then_inc(S_["norm_in"], 16)
            sp.dma_start(x_in[1], x_rows(1)).then_inc(S_["x_tile1"], 16)
            sp.dma_start(par[:], io["params"]).then_inc(S_["const_in"], 16)
            sp.dma_start(gain[:].rearrange("p a d -> p (a d)"), io["qk_gain"].partition_broadcast(P)).then_inc(
                S_["const_in"], 16)
            sp.dma_start(st_rows[0:24, :], io["state_conv"]).then_inc(S_["const_in"], 16)
            sp.dma_start(st_rows[24:32, :], io["state_lru"]).then_inc(S_["const_in"], 16)
            for t in range(2, NT + 1):
                sp.wait_ge(S_["x_turned_b"], t - 1)
                sp.dma_start(x_in[t % 2][0:tile_rows(t), :], x_rows(t)).then_inc(S_[f"x_tile{t % 2}"], 16)
                if t == 3:
                    load_w(1)
            sp.dma_start(cr[:], io["c_ret"]).then_inc(S_["cr_in"], 16)
            for hd in range(H):
                if hd > 0:
                    sp.wait_ge(S_["stored_ret"], 32 * hd)
                sp.dma_start(s0[:], io["state_ret"][:, hd].rearrange("b d e -> d b e")).then_inc(S_["s0_in"], 16)
                for u in ((2, 3, 4), (5, 6), (7,), (8,))[hd]:
                    load_w(u)
                if hd == 0:
                    for name, out in (("cache_k", "s_k"), ("cache_v", "s_v")):
                        store(io[out][:, 0:WINDOW - DS], io[name][:, DS:WINDOW], "stored_cache")
                sp.wait_ge(S_["s_set"], 9 * hd + 8)
                store(io["p_ret"][hd], S[:, hd % 2, :], "stored_ret")
                sp.wait_ge(S_["s2_set"], hd + 1)
                store(io["s_ret"][:, hd].rearrange("b d e -> d b e"), s0[:], "stored_ret")
            sp.wait_ge(S_["mix_a"], 36)
            sp.wait_ge(S_["stored_ret"], 32 * H)
            sp.dma_start(wg[:].rearrange("p a h n -> p (a h n)"), io["w_gates"]).then_inc(S_["wg_in"], 16)
            for u in range(9, 13):
                load_w(u)
            sp.wait_ge(S_["lru_set"], H)
            sp.dma_start(cc[:], io["c_att"]).then_inc(S_["cc_in"], 16)
            sp.dma_start(cache[:], io["cache_k"][:, :, 0].rearrange("b w d -> w b d")).then_inc(
                S_["kcache_in"], 16)
            load_w(13)
            load_w(14)
            sp.wait_ge(S_["tails_copied"], 1)
            store(io["s_conv"], tail_rows[0:24, :], "stored_tails")
            store(io["s_lru"], tail_rows[24:32, :], "stored_tails")
            store(io["p_conv"], tail_rows[32:35, :], "stored_tails")
            store(io["p_lru"], tail_rows[35:36, :], "stored_tails")
            for half in range(2):
                if half:
                    sp.wait_ge(S_["sav_done"], 1)
                    sp.dma_start(cache[:], io["cache_k"][:, :, 1].rearrange("b w d -> w b d")).then_inc(
                        S_["kcache_in"], 16)
                for t in (NT - 1, NT):
                    n9 = 9 * half + t
                    sp.wait_ge(S_["kn_set"], n9 + 1)
                    if t < NT:
                        store(io["p_k"][:, half], kn[:, n9 % 2, :], "stored_kv")
                        store(io["p_v"][:, half], v_c[:, half, t, :], "stored_kv")
                        continue
                    for b in range(DB):
                        rows = slice(b * DS, (b + 1) * DS)
                        store(io["s_k"][b, WINDOW - DS:WINDOW, half], kn[rows, n9 % 2, :], "stored_kv")
                        store(io["s_v"][b, WINDOW - DS:WINDOW, half], v_c[rows, half, t, :], "stored_kv")
                load_w(15 + 2 * half)
                sp.wait_ge(S_["kc_turned"], 2 * half + 2)
                sp.dma_start(cache[:], io["cache_v"][:, :, half].rearrange("b w d -> w b d")).then_inc(
                    S_["vcache_in"], 16)
                if half == 0:
                    load_w(16)
            sp.wait_ge(S_["w_hi_set"], NU)
            sp.wait_ge(S_["w_lo_set"], NU)
            for k in range(KM):
                if k >= 2:
                    sp.wait_ge(S_["w_hi_set"], NU + k - 1)
                    sp.wait_ge(S_["w_lo_set"], NU + k - 1)
                sp.dma_start(raw[:, (k % 2) * D:(k % 2 + 1) * D], io["w_out"][k * P:(k + 1) * P, :]).then_inc(
                    S_[f"wo_in{k % 2}"], 16)
                if k == 1:
                    sp.wait_ge(S_["m_hi_set"], 1)
                    for t in range(2):
                        sp.dma_start(x_res[:, t, :], x_rows(t)).then_inc(S_[f"x_again{t}"], 16)
            for t in range(NT + 1):
                sp.wait_ge(S_["y_set"], 2 * t + 2)
                if t < NT:
                    store(io["y_prompt"][t * P:(t + 1) * P, :], y_out[:, t % 2, :], f"stored_y{t % 2}")
                else:
                    store(io["y_sample"], y_out[0:NS, t % 2, :], f"stored_y{t % 2}")
                if t + 2 <= NT:
                    sp.dma_start(x_res[0:tile_rows(t + 2), t % 2, :], x_rows(t + 2)).then_inc(
                        S_[f"x_again{t % 2}"], 16)
            for name, n in n_stores.items():
                sp.wait_ge(S_[name], n)

        RET_UNIT = {2: 0, 4: 1, 5: 2, 6: 3}
        LRU_AT = {
            "conv": {(8, 6): 0, (9, 0): 1, (9, 6): 2, (10, 0): 3},
            "gates": {(8, 10): 0, (9, 4): 1, (10, 1): 2, (10, 7): 3},
            "sig": {(8, 10): 0, (9, 4): 1, (10, 1): 2, (10, 7): 3},
            "m2": {(9, 1): 0, (9, 7): 1, (10, 3): 2, (10, 9): 3},
            "sqrt": {(9, 2): 0, (9, 8): 1, (10, 4): 2, (10, 10): 3},
            "scan": {(9, 3): 0, (9, 9): 1, (10, 5): 2, (10, 11): 3},
        }
        TAILS_AT = (12, 10)

        def att_slot(u, s):
            if u in (13, 15):
                return (u - 13) // 2, s
            if u == 14:
                return 0, s + 18
            if u == 16:
                return 1, s + 18
            if u == 17 and s < 6:
                return 1, s + 30
            return None

        @block.tensor
        def _(pe):
            def three_pass(out, a_hi, a_lo, b_hi, b_lo, first, last):
                pe.matmul(out, a_lo, b_hi, start=first, stop=False)
                pe.matmul(out, a_hi, b_lo, start=False, stop=False)
                return pe.matmul(out, a_hi, b_hi, start=False, stop=last)

            def group_half(u, j, half):
                g = FIRST_GROUP[u] + j
                bank = pb[g % 3]
                if half == 0:
                    if j == 0:
                        pe.wait_ge(S_["w_lo_set"], u + 1)
                        pe.wait_ge(S_["w_hi_set"], u + 1)
                    if g >= 3:
                        name, n = freed(*GROUPS[g - 3])
                        pe.wait_ge(S_[name], n)
                for k in range(4 * half, 4 * half + 4):
                    if UNITS[u][0] in TOKEN_MAJOR:
                        n = tile_rows(j)
                        cols = chunk_cols(j)
                        w = [w_part(u % 2, i)[:, k * UNIT:(k + 1) * UNIT] for i in range(2)]
                        mm = three_pass(bank[0:n, 0:UNIT], h_hi[:, k, cols], h_lo[:, k, cols], w[0], w[1],
                                        k == 0, k == KD - 1)
                    else:
                        mt, c = j // 3, j % 3
                        cols = slice(c * CH, (c + 1) * CH)
                        w = [w_part(u % 2, i)[:, k * UNIT + mt * P:k * UNIT + (mt + 1) * P] for i in range(2)]
                        mm = three_pass(bank[:, 0:CH], w[0], w[1], h_hi[:, k, cols], h_lo[:, k, cols],
                                        k == 0, k == KD - 1)
                if half == 1:
                    mm.then_inc(S_["proj_done"], 1)

            def turn_x(t):
                n = tile_rows(t)
                pe.wait_ge(S_["x_scaled"], t + 1)
                for q in range(2):
                    bank = bb[2 * (t % 2) + q]
                    if t >= 2:
                        pe.wait_ge(S_["h_lo_set"], 2 * (t - 2) + q + 1)
                    for i in range(4):
                        k = 4 * q + i
                        mm = pe.transpose(bank[:, i * P:i * P + n], x_in[t % 2][0:n, k * P:(k + 1) * P],
                                          ident[0:n, 0:n])
                    mm.then_inc(S_["x_turned_b" if q else "x_turned_a"], 1)

            def ret_one(m):
                hd, c = divmod(m, 9)
                n, cols = tile_rows(c), chunk_cols(c)
                if c == 0:
                    pe.wait_ge(S_["act_freed"], freed(UNITS.index(("qk", hd)), 5)[1])
                if m == 0:
                    pe.wait_ge(S_["h_lo_set"], 2 * NT + 2)
                if m > 0:
                    pe.wait_ge(S_["masked"], m)
                pe.matmul(bb[0][0:n, 0:n], qk[hd][:, 1, cols], qk[hd][:, 0, cols], start=True,
                          stop=True).then_inc(S_["scores_done"], 1)
                if m > 0:
                    pe.wait_ge(S_["kdec_set"], m)
                pe.transpose(bb[1][0:n, 0:P], qk[hd][:, 1, cols], ident[:]).then_inc(S_["kturn_done"], 1)

            def ret_two(m):
                hd, c = divmod(m, 9)
                n = tile_rows(c)
                v = v_tok[0:n, hd // 2, c, (hd % 2) * DH:(hd % 2 + 1) * DH]
                if c == 0:
                    pe.wait_ge(S_["act_freed"], freed(UNITS.index(("v", hd // 2)), 8)[1])
                pe.wait_ge(S_["masked"], m + 1)
                pe.wait_ge(S_["qdec_set"], m + 1)
                if m > 0:
                    pe.wait_ge(S_["o_set"], m)
                o = bb[2]
                if c < NT:
                    mm = pe.matmul(o[:, 0:DH], sT[:, m % 2, :], v, start=True, stop=(c == 0))
                    if c > 0:
                        pe.wait_ge(S_["s_set"], m)
                        mm = pe.matmul(o[:, 0:DH], q_dec[:, m % 2, :], S[:, hd % 2, :], start=False, stop=True)
                else:
                    pe.wait_ge(S_["s0_in"], 16 * (hd + 1))
                    mm = pe.matmul(o[:, 0:NS], v, sT[0:n, m % 2, 0:n], start=True, stop=False,
                                   skip_group_check=True)
                    for b in range(DB):
                        cols = slice(b * DS, (b + 1) * DS)
                        mm = pe.matmul(o[:, cols], s0[:, b, :], q_dec[:, m % 2, cols], start=False,
                                       stop=(b == DB - 1), skip_group_check=True)
                mm.then_inc(S_["o_done"], 1)
                pe.wait_ge(S_["kdec_set"], m + 1)
                if m > 0:
                    pe.wait_ge(S_["s_set"], m)
                if c == 0 and hd > 0:
                    pe.wait_ge(S_["s2_set"], hd)
                if c < NT:
                    mm = pe.matmul(bb[3][:, 0:DH], k_dec[:, m % 2, :], v, start=True, stop=True)
                else:
                    pe.wait_ge(S_["vsel_set"], hd + 1)
                    mm = pe.matmul(bb[3][:, :], k_dec[0:n, m % 2, :],
                                   v_sel[:, 0:4, :].rearrange("p b d -> p (b d)"), start=True, stop=True)
                mm.then_inc(S_["kv_done"], 1)

            def ret_three(m):
                hd, c = divmod(m, 9)
                if c < NT:
                    pe.wait_ge(S_["o_set"], m + 1)
                    if m > 0:
                        pe.wait_ge(S_["mix_a"], m)
                    pe.transpose(bb[4][:, 0:P], o_nrm[:, m % 2, :], ident[:]).then_inc(S_["oT_done"], 1)
                else:
                    pe.wait_ge(S_["o_ss"], m + 1)
                    pe.wait_ge(S_["mix_a"], m)
                    pe.wait_ge(S_["ones_set"], 1)
                    pe.matmul(bb[4][:, 0:NS], ones[:], o_sq[:, 0:NS], start=True, stop=True).then_inc(
                        S_["oT_done"], 1)
                    pe.wait_ge(S_["s_set"], m + 1)
                    pe.matmul(bb[3][:, :], k_dec[0:NS, m % 2, :],
                              v_sel[:, 4:8, :].rearrange("p b d -> p (b d)"), start=True,
                              stop=True).then_inc(S_["kv2_done"], 1)

            def turn_states():
                pe.wait_ge(S_["const_in"], 64)
                for f in range(H):
                    mm = pe.transpose(bb[4][:, f * NS:(f + 1) * NS], st_rows[:, f * P:(f + 1) * P],
                                      ident[0:NS, 0:NS])
                mm.then_inc(S_["st_turned"], 1)

            GATE_BANKS = [0, 1, 2, 3, 4, 0]

            def lru_gates(f):
                pe.wait_ge(S_["conv_set"], f + 1)
                if f == 0:
                    pe.wait_ge(S_["wg_in"], 16)
                    pe.wait_ge(S_["mix_a"], 36)
                for q in range(6):
                    gate, c = divmod(q, 3)
                    if q == 5:
                        pe.wait_ge(S_["gates_read"], 6 * f + 1)
                    elif f > 0:
                        pe.wait_ge(S_["gates_read"], 6 * f)
                    pe.matmul(bb[GATE_BANKS[q]][:, 0:CH], wg[:, gate, f, :], cv[:, f % 2, c * CH:(c + 1) * CH],
                              start=True, stop=True).then_inc(S_["gates_done"], 1)

            def turn_tails():
                pe.wait_ge(S_["lru_set"], H)
                pe.wait_ge(S_["gates_read"], 24)
                for f in range(H):
                    mm = pe.transpose(bb[4][0:36, f * P:(f + 1) * P], tails[:, f, :], ident[:])
                mm.then_inc(S_["tails_turned"], 1)

            def turn_k(n9):
                t = n9 % 9
                n = tile_rows(t)
                pe.wait_ge(S_["kn_set"], n9 + 1)
                if n9 > 0:
                    pe.wait_ge(S_["kT_set"], n9)
                    if n9 >= 9:
                        pe.wait_ge(S_["qT_set"], 9)
                else:
                    pe.wait_ge(S_["gates_read"], 24)
                pe.transpose(bb[0][:, 0:n], kn[0:n, n9 % 2, :], ident[0:n, 0:n]).then_inc(S_["kT_done"], 1)

            def att_q(n9):
                t = n9 % 9
                n = tile_rows(t)
                pe.wait_ge(S_["qn_set"], n9 + 1)
                pe.wait_ge(S_["kT_set"], 9 * (n9 // 9) + 9)
                if n9 > 0:
                    pe.wait_ge(S_["qT_set"], n9)
                for g in range(2):
                    mm = pe.transpose(bb[0][:, g * n:(g + 1) * n], qn[0:n, n9 % 2, g * DH:(g + 1) * DH],
                                      ident[0:n, 0:n])
                mm.then_inc(S_["qT_done"], 1)

            def att_scores(half, t):
                n8 = 8 * half + t
                pe.wait_ge(S_["qT_set"], 9 * half + t + 1)
                if n8 > 0:
                    pe.wait_ge(S_["biased"], n8)
                for g in range(2):
                    lo = P if t == 0 else 0
                    mm = pe.matmul(bb[1][:, g * 2 * P + lo:(g + 1) * 2 * P],
                                   qT[:, (9 * half + t) % 2, g * P:(g + 1) * P],
                                   kT[:, half, (t - 1) * P + lo:(t + 1) * P], start=(g == 0), stop=True,
                                   skip_group_check=True)
                mm.then_inc(S_["sc_done"], 1)

            def att_turn(half, t):
                n8 = 8 * half + t
                pe.wait_ge(S_["pr_set"], n8 + 1)
                if n8 > 0:
                    pe.wait_ge(S_["pT_set"], n8)
                for kt in range(1 if t == 0 else 0, 2):
                    for g in range(2):
                        mm = pe.transpose(bb[2][:, (kt * 2 + g) * P:(kt * 2 + g + 1) * P],
                                          pr[:, n8 % 2, g, kt * P:(kt + 1) * P], ident[:])
                mm.then_inc(S_["pT_done"], 1)

            def att_values(half, t):
                n8 = 8 * half + t
                pe.wait_ge(S_["pT_set"], n8 + 1)
                if n8 > 0:
                    pe.wait_ge(S_["mix_c"], n8)
                for kt in range(1 if t == 0 else 0, 2):
                    mm = pe.matmul(bb[3][:, 0:2 * P], v_c[:, half, t - 1 + kt, :],
                                   pT[:, n8 % 2, kt * 2 * P:(kt + 1) * 2 * P], start=(kt == 0 or t == 0),
                                   stop=(kt == 1))
                mm.then_inc(S_["av_done"], 1)

            def cache_turn(half, q):
                pe.wait_ge(S_["kcache_in"], 16 * (half + 1))
                if half == 0 and q == 0:
                    pe.wait_ge(S_["tails_copied"], 1)
                if q == 1:
                    pe.wait_ge(S_["kc_copied"], 2 * half + 1)
                if half == 1 and q == 0:
                    pe.wait_ge(S_["smix_c"], 1)
                for i in range(4):
                    mm = pe.transpose(bb[4][:, i * P:(i + 1) * P], cache[:, 4 * q + i, :], ident[:])
                mm.then_inc(S_["kc_turned"], 1)

            def sample_q(half):
                return qT[:, (9 * half + NT) % 2, 0:2 * NS].rearrange("p (g b i) -> p b g i", g=2, b=DB)

            def samp_scores(half):
                pe.wait_ge(S_["qT_set"], 9 * half + 9)
                pe.wait_ge(S_["kc_copied"], 2 * half + 2)
                q = sample_q(half)
                for b in range(DB):
                    pe.matmul(bb[4][:, 8 * b:8 * b + 8], kcT[:, b, :], q[:, b], start=(b == 0), stop=True,
                              skip_group_check=True)
                mm = pe.matmul(bb[4][0:NS, 2 * NS:4 * NS], kT[:, half, SEQ:TOK], q, start=False, stop=True,
                               skip_group_check=True)
                mm.then_inc(S_["ssT_done"], 1)

            def samp_turn(half):
                pe.wait_ge(S_["ssT_set"], half + 1)
                pe.transpose(bb[4][0:64, 0:P], kcT[:, 0, 0:64], ident[:])
                pe.transpose(bb[4][0:64, P:P + NS], kcT[0:NS, 0, 64:128], ident[0:NS, 0:NS]).then_inc(
                    S_["ss_done"], 1)

            def samp_pturn(half):
                pe.wait_ge(S_["spr_set"], half + 1)
                ps = kcT[0:64, 2, :]
                pn = kcT[0:64, 3, 0:NS]
                pe.transpose(bb[4][:, 0:64], ps, ident[0:64, 0:64])
                pe.transpose(bb[4][0:NS, 64:128], pn, ident[0:64, 0:64]).then_inc(S_["spT_done"], 1)

            def samp_values(half):
                pe.wait_ge(S_["spT_set"], half + 1)
                pe.wait_ge(S_["vcache_in"], 16 * (half + 1))
                pe.matmul(bb[4][:, 0:64], v_c[0:NS, half, NT, :], kcT[0:NS, 4, 64:128], start=True, stop=False,
                          skip_group_check=True)
                for b in range(DB):
                    mm = pe.matmul(bb[4][:, 8 * b:8 * b + 8], cache[:, b, :], kcT[:, 4, 8 * b:8 * b + 8],
                                   start=False, stop=(b == DB - 1), skip_group_check=True)
                mm.then_inc(S_["sav_done"], 1)

            def att_side(half, s):
                if s % 2 == 1 and 0 <= (s - 3) // 2 <= NT and s >= 3:
                    att_q(9 * half + (s - 3) // 2)
                if s % 2 == 0 and 0 <= (s - 4) // 2 < NT:
                    att_scores(half, (s - 4) // 2)
                if s % 2 == 1 and 0 <= (s - 7) // 2 < NT:
                    att_turn(half, (s - 7) // 2)
                if s % 2 == 0 and 0 <= (s - 10) // 2 < NT:
                    att_values(half, (s - 10) // 2)
                if s in (18, 19):
                    cache_turn(half, s - 18)
                if s == 22:
                    samp_scores(half)
                if s == 24:
                    samp_turn(half)
                if s == 28:
                    samp_pturn(half)
                if s == 30:
                    samp_values(half)

            def side(u, s):
                if u in RET_UNIT:
                    base = 9 * RET_UNIT[u]
                    if 2 <= s < 11:
                        ret_three(base + s - 2)
                    if 1 <= s < 10:
                        ret_two(base + s - 1)
                    if s < 9:
                        ret_one(base + s)
                if u == 1 and s == 2:
                    turn_states()
                if (u, s) in LRU_AT["gates"]:
                    lru_gates(LRU_AT["gates"][u, s])
                if (u, s) == TAILS_AT:
                    turn_tails()
                if att_slot(u, s):
                    att_side(*att_slot(u, s))
                if UNITS[u][0] == "kvC" and s % 2 == 1 and s >= 3:
                    turn_k(9 * UNITS[u][1] + (s - 3) // 2)

            pe.wait_ge(S_["norm_in"], 32)
            turn_x(0)
            for u in range(NU):
                for j in range(n_groups(u)):
                    if u == 0:
                        if j < NT:
                            turn_x(j + 1)
                        pe.wait_ge(S_["h_hi_set"], 2 * j + 2)
                        pe.wait_ge(S_["h_lo_set"], 2 * j + 2)
                    for half in range(2):
                        group_half(u, j, half)
                        side(u, 2 * j + half)
                if UNITS[u][0] == "kvC":
                    turn_k(9 * UNITS[u][1] + 8)

            for t in range(NT + 1):
                n = tile_rows(t)
                pe.wait_ge(S_["m_lo_set"], t + 1)
                pe.wait_ge(S_["m_hi_set"], t + 1)
                if t >= 2:
                    pe.wait_ge(S_["y_set"], 2 * t - 2)
                for k in range(KM):
                    if t == 0:
                        pe.wait_ge(S_["w_hi_set"], NU + k + 1)
                        pe.wait_ge(S_["w_lo_set"], NU + k + 1)
                    for q in range(2):
                        mm = three_pass(bb[2 * (t % 2) + q][0:n, :], m_hi[:, t % 2, k, 0:n], m_lo[:, t % 2, k, 0:n],
                                        wo_hi[:, k, q * 512:(q + 1) * 512], wo_lo[:, k, q * 512:(q + 1) * 512],
                                        k == 0, k == KM - 1)
                        if k == KM - 1:
                            mm.then_inc(S_["y_done"], 1)

        @block.scalar
        def _(act):
            def w_hi(u):
                act.wait_ge(S_["raw_in"], 16 * (u + 1))
                if u >= 2:
                    act.wait_ge(S_["proj_done"], FIRST_GROUP[u - 1])
                act.activation(w_part(u % 2, 0), raw[:], ACT.Copy).then_inc(S_["w_hi_set"], 1)

            def x_stat(t):
                n = tile_rows(t)
                act.wait_ge(S_[f"x_tile{t % 2}"], 16 * (t // 2 + 1))
                act.activation(x_sq[0:n, :], x_in[t % 2][0:n, :], ACT.Square,
                               accum_out=stat[0:n, t % 2:t % 2 + 1]).then_inc(S_["x_ss"], 1)

            def x_hi(t):
                n = tile_rows(t)
                for q in range(2):
                    act.wait_ge(S_["x_turned_b" if q else "x_turned_a"], t + 1)
                    act.activation(h_hi[:, 4 * q:4 * q + 4, chunk_cols(t)],
                                   bb[2 * (t % 2) + q][:, :].rearrange("p (k n) -> p k n", k=4)[:, :, 0:n],
                                   ACT.Copy).then_inc(S_["h_hi_set"], 1)

            def evacuate(u, j):
                kind, i = UNITS[u]
                g = FIRST_GROUP[u] + j
                act.wait_ge(S_["proj_done"], g + 1)
                bank = pb[g % 3]
                mt, c = j // 3, j % 3
                cols = slice(c * CH, (c + 1) * CH)
                if kind == "v":
                    n = tile_rows(j)
                    ins = act.activation(v_tok[0:n, i, j, :], bank[0:n, 0:UNIT], ACT.Copy)
                elif kind == "qk":
                    if j == 0 and i >= 2:
                        act.wait_ge(S_["mix_a"], 9 * (i - 1))
                    ins = act.activation(qk[i][:, mt, cols], bank[:, 0:CH], ACT.Copy)
                elif kind in ("gB", "gC"):
                    if kind == "gC" and i == 0 and j == 0:
                        act.wait_ge(S_["mix_a"], 36)
                    row = (4 if kind == "gB" else 8) + 2 * i + mt
                    ins = act.activation(mixed[:, row, cols], bank[:, 0:CH], ACT.Silu)
                elif kind == "gA":
                    e = 6 * i + j
                    if e == 0:
                        act.wait_ge(S_["smix_c"], 1)
                    if e >= 2:
                        act.wait_ge(S_["mix_g"], e - 1)
                    ins = act.activation(gate_tmp[:, e % 2, :], bank[:, 0:CH], ACT.Silu)
                elif kind == "xb":
                    f = 2 * i + mt
                    if f >= 2:
                        act.wait_ge(S_["conv_set"], f - 1)
                    if f == 0 and j == 0:
                        act.wait_ge(S_["mix_a"], 36)
                        act.wait_ge(S_["stored_ret"], 32 * H)
                    n = min(CH, SEQ - c * CH)
                    if c == 2:
                        act.activation(xb[:, f % 2, 3 + SEQ:].rearrange("p (b i) -> p b i", b=DB)[:, :, 3:7],
                                       bank[:, n:CH].rearrange("p (b i) -> p b i", b=DB), ACT.Copy).then_inc(
                                           S_["xb_set"], 1)
                    ins = act.activation(xb[:, f % 2, 3 + c * CH:3 + c * CH + n], bank[:, 0:n], ACT.Copy)
                ins.then_inc(S_["act_freed"], 1)

            def ret_norm(m):
                hd, c = divmod(m, 9)
                act.wait_ge(S_["o_done"], m + 1)
                if c == 0 and hd > 0:
                    act.wait_ge(S_["oT_done"], m)
                if c < NT:
                    act.activation(o_sq[:, 0:P], bb[2][:, 0:P], ACT.Square,
                                   accum_out=stat[:, 4 + m % 2:5 + m % 2]).then_inc(S_["o_ss"], 1)
                    act.wait_ge(S_["o_pow"], m + 1)
                    if m >= 2:
                        act.wait_ge(S_["mix_a"], m - 1)
                    act.activation(o_nrm[:, m % 2, :], bb[2][:, 0:P], ACT.Copy,
                                   scale=stat[:, 8 + m % 2:9 + m % 2]).then_inc(S_["o_set"], 1)
                else:
                    act.activation(o_sq[:, 0:NS], bb[2][:, 0:NS], ACT.Square).then_inc(S_["o_ss"], 1)
                    act.wait_ge(S_["mix_a"], m - 1)
                    act.activation(o_nrm[:, m % 2, 0:NS], bb[2][:, 0:NS], ACT.Copy).then_inc(S_["o_set"], 1)

            def lru_sig(f):
                dst = (rg, ig)
                for q in range(6):
                    gate, c = divmod(q, 3)
                    if q == 0 and f > 0:
                        act.wait_ge(S_["lru_set"], f)
                    act.wait_ge(S_["gates_done"], 6 * f + q + 1)
                    col = PAR["b_r" if gate == 0 else "b_i"] + f
                    act.activation(dst[gate][:, c * CH:(c + 1) * CH], bb[[0, 1, 2, 3, 4, 0][q]][:, 0:CH],
                                   ACT.Sigmoid, bias=par[:, col:col + 1]).then_inc(S_["gates_read"], 1)
                act.wait_ge(S_["gates_read"], 6 * f + 6)
                if f == 0:
                    act.wait_ge(S_["decay_set"], 1)
                act.activation(aa[:], rg[:], ACT.Exp, scale=sp_t[:, 6, f:f + 1]).then_inc(S_["exp_set"], 1)
                act.activation(tt[:], rg[:], ACT.Tanh, scale=sp_t[:, 7, f:f + 1]).then_inc(S_["exp_set"], 1)

            def lru_sqrt(f):
                act.wait_ge(S_["m2_set"], f + 1)
                act.activation(rg[:], tt[:], ACT.Sqrt, scale=2.0).then_inc(S_["m_set"], 1)

            def k_stat(u, j):
                half = UNITS[u][1]
                n = tile_rows(j)
                g, n9 = FIRST_GROUP[u] + j, 9 * half + j
                act.wait_ge(S_["proj_done"], g + 1)
                if u == 12 and j == 0:
                    act.wait_ge(S_["lru_set"], H)
                if n9 > 0:
                    act.wait_ge(S_["k_ss"], 2 * n9)
                if half == 1:
                    act.wait_ge(S_["q_ss"], 2 * (NT + 1))
                bank = pb[g % 3]
                act.activation(junk[0:n, 0:DH], bank[0:n, 0:DH], ACT.Square,
                               accum_out=stat[0:n, 12 + n9 % 2:13 + n9 % 2]).then_inc(S_["k_ss"], 1)
                act.activation(v_c[0:n, half, j, :], bank[0:n, DH:2 * DH], ACT.Copy).then_inc(S_["k_ss"], 1)

            def k_copy(n9):
                half, t = divmod(n9, 9)
                n = tile_rows(t)
                act.wait_ge(S_["kT_done"], n9 + 1)
                act.activation(kT[:, half, chunk_cols(t)], bb[0][:, 0:n], ACT.Copy).then_inc(S_["kT_set"], 1)

            def q_stat(u, j):
                half = UNITS[u][1]
                n = tile_rows(j)
                g, n9 = FIRST_GROUP[u] + j, 9 * half + j
                act.wait_ge(S_["proj_done"], g + 1)
                act.wait_ge(S_["k_ss"], 2 * (NT + 1) * (half + 1))
                if n9 > 0:
                    act.wait_ge(S_["q_ss"], 2 * n9)
                for i in range(2):
                    act.activation(junk[0:n, i * DH:(i + 1) * DH], pb[g % 3][0:n, i * DH:(i + 1) * DH], ACT.Square,
                                   accum_out=stat[0:n, 20 + 2 * (n9 % 2) + i:21 + 2 * (n9 % 2) + i]).then_inc(
                                       S_["q_ss"], 1)

            def q_copy(n9):
                n = tile_rows(n9 % 9)
                act.wait_ge(S_["qT_done"], n9 + 1)
                if n9 >= 2:
                    h2, t2 = divmod(n9 - 2, 9)
                    if t2 < NT:
                        act.wait_ge(S_["sc_done"], 8 * h2 + t2 + 1)
                    else:
                        act.wait_ge(S_["ssT_done"], h2 + 1)
                act.activation(qT[:, n9 % 2, 0:2 * n], bb[0][:, 0:2 * n], ACT.Copy).then_inc(S_["qT_set"], 1)

            def att_exp(half, t):
                n8 = 8 * half + t
                act.wait_ge(S_["mx_set"], n8 + 1)
                lo = P if t == 0 else 0
                c = 32 + 8 * (n8 % 2)
                for g in range(2):
                    act.activation(pr[:, n8 % 2, g, lo:], pr[:, n8 % 2, g, lo:], ACT.Exp,
                                   bias=stat[:, c + g:c + g + 1],
                                   accum_out=stat[:, c + 4 + g:c + 5 + g]).then_inc(S_["ex_set"], 1)
                act.activation(stat[:, c + 2:c + 4], stat[:, c + 2:c + 4], ACT.Exp).then_inc(S_["ex_set"], 1)

            def att_pcopy(half, t):
                n8 = 8 * half + t
                act.wait_ge(S_["pT_done"], n8 + 1)
                if n8 >= 2:
                    act.wait_ge(S_["av_done"], n8 - 1)
                lo = 2 * P if t == 0 else 0
                act.activation(pT[:, n8 % 2, lo:], bb[2][:, lo:], ACT.Copy).then_inc(S_["pT_set"], 1)

            def cache_copy(half, q):
                act.wait_ge(S_["kc_turned"], 2 * half + q + 1)
                act.activation(kcT[:, 4 * q:4 * q + 4, :], bb[4][:, :].rearrange("p (b n) -> p b n", b=4),
                               ACT.Copy).then_inc(S_["kc_copied"], 1)

            def samp_copy(half):
                act.wait_ge(S_["ssT_done"], half + 1)
                act.activation(kcT[:, 0, 0:64], bb[4][:, 0:64], ACT.Copy).then_inc(S_["ssT_part"], 1)
                act.activation(kcT[0:NS, 0, 64:128], bb[4][0:NS, 64:128], ACT.Copy).then_inc(S_["ssT_set"], 1)

            def samp_exp(half):
                act.wait_ge(S_["smx_set"], half + 1)
                act.activation(kcT[0:64, 2:4, :].rearrange("p a n -> p (a n)")[:, 0:AKEYS],
                               kcT[0:64, 5:7, :].rearrange("p a n -> p (a n)")[:, 0:AKEYS], ACT.Exp,
                               bias=stat[0:64, 48:49], accum_out=stat[0:64, 50:51]).then_inc(S_["sex_set"], 1)
                act.activation(stat[0:64, 49:50], stat[0:64, 49:50], ACT.Exp).then_inc(S_["sex_set"], 1)

            def samp_pcopy(half):
                act.wait_ge(S_["spT_done"], half + 1)
                act.activation(kcT[:, 4, 0:64], bb[4][:, 0:64], ACT.Copy).then_inc(S_["spT_part"], 1)
                act.activation(kcT[0:NS, 4, 64:128], bb[4][0:NS, 64:128], ACT.Copy).then_inc(S_["spT_set"], 1)

            def att_side(half, s):
                if s % 2 == 1 and s >= 3 and (s - 3) // 2 <= NT:
                    q_copy(9 * half + (s - 3) // 2)
                if s % 2 == 1 and 0 <= (s - 5) // 2 < NT:
                    att_exp(half, (s - 5) // 2)
                if s % 2 == 0 and 0 <= (s - 8) // 2 < NT:
                    att_pcopy(half, (s - 8) // 2)
                if s in (18, 19):
                    cache_copy(half, s - 18)
                if s == 23:
                    samp_copy(half)
                if s == 26:
                    samp_exp(half)
                if s == 29:
                    samp_pcopy(half)

            def side(u, s):
                if (u, s) == (1, 4):
                    lam_exp()
                if u in RET_UNIT and 1 <= s < 10:
                    ret_norm(9 * RET_UNIT[u] + s - 1)
                if (u, s) in LRU_AT["sig"]:
                    lru_sig(LRU_AT["sig"][u, s])
                if (u, s) in LRU_AT["sqrt"]:
                    lru_sqrt(LRU_AT["sqrt"][u, s])
                if UNITS[u][0] == "kvC" and s % 2 == 1 and s >= 3:
                    k_copy(9 * UNITS[u][1] + (s - 3) // 2)
                if att_slot(u, s):
                    att_side(*att_slot(u, s))
                if (u, s) == (TAILS_AT[0], TAILS_AT[1] + 1):
                    act.wait_ge(S_["tails_turned"], 1)
                    act.activation(tail_rows[:], bb[4][0:36, :], ACT.Copy).then_inc(S_["tails_copied"], 1)

            def lam_exp():
                act.wait_ge(S_["const_in"], 64)
                act.activation(sp_t[:, 0, :], par[:, PAR["lam"]:PAR["lam"] + H], ACT.Abs).then_inc(
                    S_["chain_a"], 1)
                act.wait_ge(S_["chain_a"], 1)
                act.activation(sp_t[:, 1, :], sp_t[:, 0, :], ACT.Exp, scale=-1.0).then_inc(S_["lam_exp"], 1)

            x_stat(0)
            w_hi(0)
            for u in range(NU):
                for j in range(n_groups(u)):
                    if u == 0:
                        if j == 0:
                            x_hi(0)
                        if j < NT:
                            x_stat(j + 1)
                            x_hi(j + 1)
                    side(u, 2 * j)
                    if UNITS[u][0] == "kvC":
                        k_stat(u, j)
                    elif UNITS[u][0] == "qC":
                        q_stat(u, j)
                    else:
                        evacuate(u, j)
                    side(u, 2 * j + 1)
                    if j == 2 and u + 1 < NU:
                        w_hi(u + 1)
                if UNITS[u][0] == "kvC":
                    k_copy(9 * UNITS[u][1] + 8)

            def m_high(t):
                n = tile_rows(t)
                if t == 0:
                    act.wait_ge(S_["smix_c"], 2)
                    act.wait_ge(S_["mix_g"], 12)
                    act.wait_ge(S_["mix_c"], 16)
                    act.wait_ge(S_["stored_kv"], n_stores["stored_kv"])
                if t >= 2:
                    act.wait_ge(S_["y_done"], 2 * (t - 1))
                act.activation(m_hi[:, t % 2, :, 0:n], mixed[:, :, chunk_cols(t)], ACT.Copy).then_inc(
                    S_["m_hi_set"], 1)

            m_high(0)
            for k in range(KM):
                act.wait_ge(S_[f"wo_in{k % 2}"], 16 * (k // 2 + 1))
                if k == 0:
                    act.wait_ge(S_["proj_done"], FIRST_GROUP[NU])
                act.activation(wo_hi[:, k, :], raw[:, (k % 2) * D:(k % 2 + 1) * D], ACT.Copy).then_inc(
                    S_["w_hi_set"], 1)
            for t in range(1, NT + 1):
                m_high(t)

        @block.vector
        def _(dve):
            count = [0]

            def link(ins):
                count[0] += 1
                ins.then_inc(S_["chain_v"], 1)
                dve.wait_ge(S_["chain_v"], count[0])

            def w_low(u):
                dve.wait_ge(S_["w_hi_set"], u + 1)
                dve.tensor_tensor(w_part(u % 2, 1), raw[:], w_part(u % 2, 0).bitcast(F32),
                                  ALU.subtract).then_inc(S_["w_lo_set"], 1)

            def x_scale(t):
                n = tile_rows(t)
                dve.wait_ge(S_["x_pow"], t + 1)
                if t == 0:
                    dve.wait_ge(S_["norm_in"], 32)
                dve.scalar_tensor_tensor(out=x_in[t % 2][0:n, :], in0=x_in[t % 2][0:n, :],
                                         scalar=stat[0:n, 2 + t % 2:3 + t % 2], in1=g_row[0:n, :],
                                         op0=ALU.mult, op1=ALU.mult).then_inc(S_["x_scaled"], 1)

            def x_lo(t):
                n = tile_rows(t)
                for q in range(2):
                    dve.wait_ge(S_["h_hi_set"], 2 * t + q + 1)
                    dve.tensor_tensor(h_lo[:, 4 * q:4 * q + 4, chunk_cols(t)],
                                      bb[2 * (t % 2) + q][:, :].rearrange("p (k n) -> p k n", k=4)[:, :, 0:n],
                                      h_hi[:, 4 * q:4 * q + 4, chunk_cols(t)].bitcast(F32),
                                      ALU.subtract).then_inc(S_["h_lo_set"], 1)

            def ret_mask(m):
                hd, c = divmod(m, 9)
                n = tile_rows(c)
                dve.wait_ge(S_["scores_done"], m + 1)
                if m == 0:
                    dve.wait_ge(S_["cr_in"], 16)
                if m >= 2:
                    dve.wait_ge(S_["o_done"], m - 1)
                mask = cr[:, C_MASK + hd * P:C_MASK + (hd + 1) * P] if c < NT else \
                    cr[0:NS, C_MASKS + hd * NS:C_MASKS + (hd + 1) * NS]
                dve.tensor_tensor(sT[0:n, m % 2, 0:n], bb[0][0:n, 0:n], mask, ALU.mult).then_inc(S_["masked"], 1)
                dve.wait_ge(S_["kturn_done"], m + 1)
                if m >= 2:
                    dve.wait_ge(S_["kv_done"], m - 1)
                if c < NT:
                    ins = dve.tensor_scalar(k_dec[:, m % 2, :], bb[1][:, 0:P],
                                            cr[:, C_KDEC + hd:C_KDEC + hd + 1], None, ALU.mult)
                else:
                    ins = dve.tensor_copy(k_dec[0:n, m % 2, :], bb[1][0:n, 0:P])
                ins.then_inc(S_["kdec_set"], 1)

            def ret_state(m):
                hd, c = divmod(m, 9)
                dve.wait_ge(S_["kv_done"], m + 1)
                dve.wait_ge(S_["o_done"], m + 1)
                if c == 0:
                    if hd >= 2:
                        dve.wait_ge(S_["stored_ret"], 32 * (hd - 1))
                    ins = dve.tensor_copy(S[:, hd % 2, :], bb[3][:, 0:DH])
                elif c < NT:
                    ins = dve.scalar_tensor_tensor(out=S[:, hd % 2, :], in0=S[:, hd % 2, :],
                                                   scalar=float(gammas[hd] ** P), in1=bb[3][:, 0:DH],
                                                   op0=ALU.mult, op1=ALU.add)
                else:
                    ins = samp_state(hd, 0)
                ins.then_inc(S_["s_set"], 1)

            def samp_state(hd, q):
                part = s0[:, 4 * q:4 * q + 4, :].rearrange("p b e -> p (b e)")
                return dve.scalar_tensor_tensor(out=part, in0=part, scalar=float(gammas[hd] ** DS),
                                                in1=bb[3][:, :], op0=ALU.mult, op1=ALU.add)

            def ret_mix(m):
                hd, c = divmod(m, 9)
                dve.wait_ge(S_["oT_done"], m + 1)
                g = par[:, PAR["ret_g"] + hd:PAR["ret_g"] + hd + 1]
                if c < NT:
                    dve.tensor_scalar(mixed[:, hd, chunk_cols(c)], bb[4][:, 0:P], g, None, ALU.mult).then_inc(
                        S_["mix_a"], 1)
                else:
                    dve.tensor_scalar(o_rs[:, 0, :], bb[4][:, 0:NS], 1.0 / DH, EPS, ALU.mult,
                                      ALU.add).then_inc(S_["o_ms"], 1)
                    dve.wait_ge(S_["kv2_done"], hd + 1)
                    samp_state(hd, 1).then_inc(S_["s2_set"], 1)
                    dve.wait_ge(S_["o_set"], m + 1)
                    dve.wait_ge(S_["o_pow"], m + 1)
                    dve.scalar_tensor_tensor(out=mixed[:, hd, SEQ:TOK], in0=o_nrm[:, m % 2, 0:NS], scalar=g,
                                             in1=o_rs[:, 1, :], op0=ALU.mult, op1=ALU.mult).then_inc(
                                                 S_["mix_a"], 1)

            def softplus():
                lam = par[:, PAR["lam"]:PAR["lam"] + H]
                a, y, s, s2, acc, relu = (sp_t[:, i, :] for i in range(6))
                dve.wait_ge(S_["lam_exp"], 1)
                link(dve.tensor_scalar(a, y, 2.0, None, ALU.add))
                link(dve.reciprocal(a, a))
                link(dve.tensor_tensor(s, y, a, ALU.mult))
                link(dve.tensor_tensor(s2, s, s, ALU.mult))
                link(dve.tensor_scalar(acc, s2, 2.0 / 19, 2.0 / 17, ALU.mult, ALU.add))
                for d in (15, 13, 11, 9, 7, 5, 3, 1):
                    link(dve.tensor_tensor(acc, acc, s2, ALU.mult))
                    link(dve.tensor_scalar(acc, acc, 2.0 / d, None, ALU.add))
                link(dve.tensor_tensor(acc, acc, s, ALU.mult))
                link(dve.tensor_scalar(relu, lam, -1.0, 0.0, ALU.mult, ALU.max))
                link(dve.tensor_tensor(acc, acc, relu, ALU.add))
                link(dve.tensor_scalar(sp_t[:, 6, :], acc, -LRU_C, None, ALU.mult))
                dve.tensor_scalar(sp_t[:, 7, :], acc, LRU_C, None, ALU.mult).then_inc(S_["decay_set"], 1)

            def conv(f):
                i = f % 2
                samp = xb[:, i, 3 + SEQ:].rearrange("p (b i) -> p b i", b=DB)
                if f == 0:
                    dve.wait_ge(S_["stored_ret"], 32 * H)
                if f < 2:
                    link(dve.memset(xb[:, i, 0:3], 0.0))
                link(dve.tensor_copy(samp[:, :, 0:3], st_T[:, f, 0:24].rearrange("p (b i) -> p b i", b=DB)))
                dve.wait_ge(S_["act_freed"], freed(8 + f // 2, 3 * (f % 2) + 2)[1])
                dve.wait_ge(S_["xb_set"], f + 1)
                w = [par[:, PAR["conv_w"] + 4 * j + f:PAR["conv_w"] + 4 * j + f + 1] for j in range(CONV)]
                b = par[:, PAR["conv_b"] + f:PAR["conv_b"] + f + 1]
                out_p = cv[:, i, 0:SEQ]
                out_s = cv[:, i, SEQ:TOK].rearrange("p (b i) -> p b i", b=DB)
                dve.tensor_scalar(out_p, xb[:, i, 0:SEQ], w[0], b, ALU.mult, ALU.add)
                link(dve.tensor_scalar(out_s, samp[:, :, 0:DS], w[0], b, ALU.mult, ALU.add))
                for j in range(1, CONV):
                    dve.scalar_tensor_tensor(out=out_p, in0=xb[:, i, j:j + SEQ], scalar=w[j], in1=out_p,
                                             op0=ALU.mult, op1=ALU.add)
                    last = dve.scalar_tensor_tensor(out=out_s, in0=samp[:, :, j:j + DS], scalar=w[j], in1=out_s,
                                                    op0=ALU.mult, op1=ALU.add)
                    if j < CONV - 1:
                        link(last)
                link(last)
                dve.tensor_copy(tails[:, f, 0:24].rearrange("p (b i) -> p b i", b=DB), samp[:, :, 4:7])
                dve.tensor_copy(tails[:, f, 32:35], xb[:, i, SEQ:SEQ + 3]).then_inc(S_["conv_set"], 1)

            def lru_m2(f):
                dve.wait_ge(S_["exp_set"], 2 * f + 2)
                dve.wait_ge(S_["gates_read"], 6 * f + 6)
                link(dve.tensor_tensor(cv[:, f % 2, :], ig[:], cv[:, f % 2, :], ALU.mult))
                link(dve.tensor_scalar(ig[:], tt[:], 1.0, None, ALU.add))
                link(dve.reciprocal(ig[:], ig[:]))
                dve.tensor_tensor(tt[:], tt[:], ig[:], ALU.mult).then_inc(S_["m2_set"], 1)

            def lru_scan(f):
                a_first = aa[:, SEQ:TOK].rearrange("p (b i) -> p b i", b=DB)[:, :, 0]
                u = cv[:, f % 2, :]
                u_first = u[:, SEQ:TOK].rearrange("p (b i) -> p b i", b=DB)[:, :, 0]
                dve.wait_ge(S_["m_set"], f + 1)
                link(dve.memset(rg[:, 0:1], 1.0))
                link(dve.tensor_tensor(u, u, rg[:], ALU.mult))
                link(dve.tensor_tensor(ig[:, 0:DB], a_first, st_T[:, f, 24:32], ALU.mult))
                link(dve.tensor_tensor(u_first, u_first, ig[:, 0:DB], ALU.add))
                link(dve.memset(a_first, 0.0))
                link(dve.tensor_tensor_scan(tt[:], aa[:], u, 0.0, ALU.mult, ALU.add))
                dve.tensor_copy(tails[:, f, 24:32],
                                tt[:, SEQ:TOK].rearrange("p (b i) -> p b i", b=DB)[:, :, DS - 1])
                dve.tensor_copy(tails[:, f, 35:36], tt[:, SEQ - 1:SEQ])
                dve.wait_ge(S_["act_freed"], freed(7, 5)[1])
                dve.tensor_tensor(mixed[:, H + f, :], mixed[:, H + f, :], tt[:], ALU.mult).then_inc(
                    S_["lru_set"], 1)

            def k_norm(u, j):
                half = UNITS[u][1]
                n = tile_rows(j)
                g, n9 = FIRST_GROUP[u] + j, 9 * half + j
                dve.wait_ge(S_["k_pow"], n9 + 1)
                dve.wait_ge(S_["k_ss"], 2 * n9 + 2)
                if n9 >= 2:
                    dve.wait_ge(S_["kT_done"], n9 - 1)
                if n9 == 9:
                    dve.wait_ge(S_["stored_kv"], 16 * (2 + 2 * DB))
                dve.scalar_tensor_tensor(out=kn[0:n, n9 % 2, :], in0=pb[g % 3][0:n, 0:DH],
                                         scalar=stat[0:n, 16 + n9 % 2:17 + n9 % 2], in1=gain[0:n, 1, :],
                                         op0=ALU.mult, op1=ALU.mult).then_inc(S_["kn_set"], 1)

            def q_norm(u, j):
                half = UNITS[u][1]
                n = tile_rows(j)
                g, n9 = FIRST_GROUP[u] + j, 9 * half + j
                dve.wait_ge(S_["q_pow"], n9 + 1)
                if n9 >= 2:
                    dve.wait_ge(S_["qT_done"], n9 - 1)
                for i in range(2):
                    c = 24 + 2 * (n9 % 2) + i
                    ins = dve.scalar_tensor_tensor(out=qn[0:n, n9 % 2, i * DH:(i + 1) * DH],
                                                   in0=pb[g % 3][0:n, i * DH:(i + 1) * DH],
                                                   scalar=stat[0:n, c:c + 1], in1=gain[0:n, 0, :],
                                                   op0=ALU.mult, op1=ALU.mult)
                    ins.then_inc(S_["qn_set" if i else "qn_half"], 1)

            def att_max(half, t):
                n8 = 8 * half + t
                lo = P if t == 0 else 0
                c = 32 + 8 * (n8 % 2)
                dve.wait_ge(S_["sc_done"], n8 + 1)
                if n8 == 0:
                    dve.wait_ge(S_["cc_in"], 16)
                if n8 >= 2:
                    dve.wait_ge(S_["pT_done"], n8 - 1)
                bias = cc[:, C_BIAS + half * 512:C_BIAS + (half + 1) * 512].rearrange("p (g n) -> p g n", g=2)
                ins = dve.scalar_tensor_tensor(out=pr[:, n8 % 2, :, lo:],
                                               in0=bb[1][:, :].rearrange("p (g n) -> p g n", g=2)[:, :, lo:],
                                               scalar=SCALE, in1=bias[:, :, lo:], op0=ALU.mult, op1=ALU.add)
                ins.then_inc(S_["biased"], 1)
                dve.wait_ge(S_["biased"], n8 + 1)
                sink = par[:, PAR["sink"] + 2 * half:PAR["sink"] + 2 * half + 2]
                link(dve.tensor_reduce(stat[:, c:c + 2], pr[:, n8 % 2, :, lo:], AX.X, ALU.max))
                link(dve.tensor_tensor(stat[:, c:c + 2], stat[:, c:c + 2], sink, ALU.max))
                link(dve.tensor_scalar(stat[:, c:c + 2], stat[:, c:c + 2], -1.0, None, ALU.mult))
                dve.tensor_tensor(stat[:, c + 2:c + 4], stat[:, c:c + 2], sink, ALU.add).then_inc(
                    S_["mx_set"], 1)

            def att_probs(half, t):
                n8 = 8 * half + t
                lo = P if t == 0 else 0
                c = 32 + 8 * (n8 % 2)
                dve.wait_ge(S_["ex_set"], 3 * n8 + 3)
                link(dve.tensor_tensor(stat[:, c + 4:c + 6], stat[:, c + 4:c + 6], stat[:, c + 2:c + 4], ALU.add))
                link(dve.reciprocal(stat[:, c + 4:c + 6], stat[:, c + 4:c + 6]))
                for g in range(2):
                    ins = dve.tensor_scalar(pr[:, n8 % 2, g, lo:], pr[:, n8 % 2, g, lo:],
                                            stat[:, c + 4 + g:c + 5 + g], None, ALU.mult)
                ins.then_inc(S_["pr_set"], 1)

            def att_mix(half, t):
                n8 = 8 * half + t
                dve.wait_ge(S_["av_done"], n8 + 1)
                m = mixed[:, 2 * H + 2 * half:2 * H + 2 * half + 2, chunk_cols(t)]
                dve.tensor_tensor(m, bb[3][:, 0:2 * P].rearrange("p (g n) -> p g n", g=2), m,
                                  ALU.mult).then_inc(S_["mix_c"], 1)

            def samp_max(half):
                dve.wait_ge(S_["ss_done"], half + 1)
                sc = kcT[0:64, 5:7, :].rearrange("p a n -> p (a n)")[:, 0:AKEYS]
                bias = cc[0:64, C_BIASS + half * AKEYS:C_BIASS + (half + 1) * AKEYS]
                sink = par[0:64, PAR["sink_s"] + half:PAR["sink_s"] + half + 1]
                link(dve.scalar_tensor_tensor(out=sc, in0=bb[4][0:64, 0:AKEYS], scalar=SCALE, in1=bias,
                                              op0=ALU.mult, op1=ALU.add))
                link(dve.tensor_reduce(stat[0:64, 48:49], sc, AX.X, ALU.max))
                link(dve.tensor_tensor(stat[0:64, 48:49], stat[0:64, 48:49], sink, ALU.max))
                link(dve.tensor_scalar(stat[0:64, 48:49], stat[0:64, 48:49], -1.0, None, ALU.mult))
                dve.tensor_tensor(stat[0:64, 49:50], stat[0:64, 48:49], sink, ALU.add).then_inc(S_["smx_set"], 1)

            def samp_probs(half):
                dve.wait_ge(S_["sex_set"], 2 * half + 2)
                link(dve.tensor_tensor(stat[0:64, 50:51], stat[0:64, 50:51], stat[0:64, 49:50], ALU.add))
                link(dve.reciprocal(stat[0:64, 50:51], stat[0:64, 50:51]))
                p = kcT[0:64, 2:4, :].rearrange("p a n -> p (a n)")[:, 0:AKEYS]
                dve.tensor_scalar(p, p, stat[0:64, 50:51], None, ALU.mult).then_inc(S_["spr_set"], 1)

            def samp_mix(half):
                dve.wait_ge(S_["sav_done"], half + 1)
                for g in range(2):
                    m = mixed[:, 2 * H + 2 * half + g, SEQ:TOK].rearrange("p (b i) -> p b i", b=DB)
                    o = bb[4][:, 0:64].rearrange("p (b g i) -> p b g i", b=DB, g=2)[:, :, g, :]
                    ins = dve.tensor_tensor(m, o, m, ALU.mult)
                    ins.then_inc(S_["smix_c" if g else "smix_half"], 1)

            def att_side(half, s):
                if s % 2 == 0 and 0 <= (s - 10) // 2 < NT:
                    att_mix(half, (s - 10) // 2)
                if s % 2 == 0 and 0 <= (s - 4) // 2 < NT:
                    att_max(half, (s - 4) // 2)
                if s % 2 == 0 and 0 <= (s - 6) // 2 < NT:
                    att_probs(half, (s - 6) // 2)
                if s == 25:
                    samp_max(half)
                if s == 27:
                    samp_probs(half)
                if s == 31:
                    samp_mix(half)

            def side(u, s):
                if u in RET_UNIT:
                    base = 9 * RET_UNIT[u]
                    if s < 9:
                        ret_mask(base + s)
                    if 1 <= s < 10:
                        ret_state(base + s - 1)
                    if 2 <= s < 11:
                        ret_mix(base + s - 2)
                if u == 1 and s == 3:
                    dve.wait_ge(S_["st_turned"], 1)
                    dve.tensor_copy(st_T[:].rearrange("p f n -> p (f n)"), bb[4][:, 0:H * NS]).then_inc(
                        S_["st_copied"], 1)
                if (u, s) == (1, 6):
                    softplus()
                if (u, s) in LRU_AT["conv"]:
                    conv(LRU_AT["conv"][u, s])
                if (u, s) in LRU_AT["m2"]:
                    lru_m2(LRU_AT["m2"][u, s])
                if (u, s) in LRU_AT["scan"]:
                    lru_scan(LRU_AT["scan"][u, s])
                if att_slot(u, s):
                    att_side(*att_slot(u, s))

            for u in range(NU):
                if u == 0:
                    x_scale(0)
                    w_low(0)
                for j in range(n_groups(u)):
                    if u == 0:
                        if j == 0:
                            x_lo(0)
                        if j < NT:
                            x_scale(j + 1)
                            x_lo(j + 1)
                    side(u, 2 * j)
                    if UNITS[u][0] == "kvC":
                        k_norm(u, j)
                    if UNITS[u][0] == "qC":
                        q_norm(u, j)
                    if UNITS[u][0] == "gA":
                        e = 6 * UNITS[u][1] + j
                        dve.wait_ge(S_["act_freed"], freed(u, j)[1])
                        row, cols = e // 3, slice((e % 3) * CH, (e % 3 + 1) * CH)
                        dve.tensor_tensor(mixed[:, row, cols], mixed[:, row, cols], gate_tmp[:, e % 2, :],
                                          ALU.mult).then_inc(S_["mix_g"], 1)
                    side(u, 2 * j + 1)
                    if j == 2 and u + 1 < NU:
                        w_low(u + 1)

            def m_low(t):
                n = tile_rows(t)
                dve.wait_ge(S_["m_hi_set"], t + 1)
                dve.tensor_tensor(m_lo[:, t % 2, :, 0:n], mixed[:, :, chunk_cols(t)],
                                  m_hi[:, t % 2, :, 0:n].bitcast(F32), ALU.subtract).then_inc(S_["m_lo_set"], 1)

            m_low(0)
            for k in range(KM):
                dve.wait_ge(S_["w_hi_set"], NU + k + 1)
                dve.tensor_tensor(wo_lo[:, k, :], raw[:, (k % 2) * D:(k % 2 + 1) * D],
                                  wo_hi[:, k, :].bitcast(F32), ALU.subtract).then_inc(S_["w_lo_set"], 1)
            for t in range(NT + 1):
                n = tile_rows(t)
                if t < NT:
                    m_low(t + 1)
                dve.wait_ge(S_[f"x_again{t % 2}"], 16 * (t // 2 + 1))
                if t >= 2:
                    dve.wait_ge(S_[f"stored_y{t % 2}"], 16 * (t // 2))
                for q in range(2):
                    cols = slice(q * 512, (q + 1) * 512)
                    dve.wait_ge(S_["y_done"], 2 * t + q + 1)
                    dve.tensor_tensor(y_out[0:n, t % 2, cols], bb[2 * (t % 2) + q][0:n, :],
                                      x_res[0:n, t % 2, cols], ALU.add).then_inc(S_["y_set"], 1)

        @block.gpsimd
        def _(pool):
            count = [0]

            def link(ins):
                count[0] += 1
                ins.then_inc(S_["chain_p"], 1)
                pool.wait_ge(S_["chain_p"], count[0])

            def root(ss, rs, n, width):
                w = ss.shape[1]
                link(pool.tensor_scalar(ss, ss, 1.0 / width, EPS, ALU.mult, ALU.add))
                return pool.tensor_tensor(rs, ss, neghalf[0:n, 0:w], ALU.pow)

            def ret_qdec(m):
                hd, c = divmod(m, 9)
                n = tile_rows(c)
                if m == 0:
                    pool.wait_ge(S_["cr_in"], 16)
                if c == 0:
                    pool.wait_ge(S_["act_freed"], freed(UNITS.index(("qk", hd)), 5)[1])
                if m >= 2:
                    pool.wait_ge(S_["o_done"], m - 1)
                dec = cr[:, C_QDEC + hd * P:C_QDEC + (hd + 1) * P] if c < NT else \
                    cr[:, C_QDECS + hd * NS:C_QDECS + (hd + 1) * NS]
                pool.tensor_tensor(q_dec[:, m % 2, 0:n], qk[hd][:, 0, chunk_cols(c)], dec, ALU.mult).then_inc(
                    S_["qdec_set"], 1)
                if c == 0:
                    pool.wait_ge(S_["act_freed"], freed(UNITS.index(("v", hd // 2)), 8)[1])
                    if hd > 0:
                        pool.wait_ge(S_["kv2_done"], hd)
                    for b in range(DB):
                        col = C_VSEL + hd * DB + b
                        ins = pool.tensor_scalar(v_sel[:, b, :],
                                                 v_tok[0:NS, hd // 2, NT, (hd % 2) * DH:(hd % 2 + 1) * DH],
                                                 cr[0:NS, col:col + 1], None, ALU.mult)
                    ins.then_inc(S_["vsel_set"], 1)

            def ret_root(m):
                hd, c = divmod(m, 9)
                if c < NT:
                    pool.wait_ge(S_["o_ss"], m + 1)
                    root(stat[:, 4 + m % 2:5 + m % 2], stat[:, 8 + m % 2:9 + m % 2], P, DH).then_inc(
                        S_["o_pow"], 1)
                else:
                    pool.wait_ge(S_["o_ms"], hd + 1)
                    pool.tensor_tensor(o_rs[:, 1, :], o_rs[:, 0, :], neghalf[:], ALU.pow).then_inc(S_["o_pow"], 1)

            link(pool.memset(neghalf[:], -0.5))
            pool.memset(ones[:], 1.0).then_inc(S_["ones_set"], 1)
            for t in range(NT + 1):
                n = tile_rows(t)
                pool.wait_ge(S_["x_ss"], t + 1)
                root(stat[0:n, t % 2:t % 2 + 1], stat[0:n, 2 + t % 2:3 + t % 2], n, D).then_inc(S_["x_pow"], 1)
            for hd in range(H):
                for c in range(NT + 2):
                    if c <= NT:
                        ret_qdec(9 * hd + c)
                    if c >= 1:
                        ret_root(9 * hd + c - 1)
            for half in range(2):
                for j in range(NT + 1):
                    n, n9 = tile_rows(j), 9 * half + j
                    pool.wait_ge(S_["k_ss"], 2 * n9 + 1)
                    root(stat[0:n, 12 + n9 % 2:13 + n9 % 2], stat[0:n, 16 + n9 % 2:17 + n9 % 2], n, DH).then_inc(
                        S_["k_pow"], 1)
                for j in range(NT + 1):
                    n, n9 = tile_rows(j), 9 * half + j
                    c = 2 * (n9 % 2)
                    pool.wait_ge(S_["q_ss"], 2 * n9 + 2)
                    root(stat[0:n, 20 + c:22 + c], stat[0:n, 24 + c:26 + c], n, DH).then_inc(S_["q_pow"], 1)


def constants():
    log_g = np.log1p(-np.power(2.0, -5.0 - np.arange(H)))
    i = np.arange(P)
    d = i[None, :] - i[:, None]
    cr = np.zeros((P, N_CR))
    for h in range(H):
        cr[:, C_MASK + h * P:C_MASK + (h + 1) * P] = np.where(d >= 0, np.exp(np.maximum(d, 0) * log_g[h]), 0) * SCALE
        cr[:, C_QDEC + h * P:C_QDEC + (h + 1) * P] = np.exp((i + 1) * log_g[h])[None, :]
        cr[:, C_KDEC + h] = np.exp((P - 1 - i) * log_g[h]) * SCALE
        t = np.arange(NS)
        same = (t[:, None] // DS) == (t[None, :] // DS)
        ds = t[None, :] - t[:, None]
        cr[:NS, C_MASKS + h * NS:C_MASKS + (h + 1) * NS] = \
            np.where(same & (ds >= 0), np.exp(np.maximum(ds, 0) * log_g[h]), 0) * SCALE
        cr[:, C_QDECS + h * NS:C_QDECS + (h + 1) * NS] = np.exp((t % DS + 1) * log_g[h])[None, :]
        for b in range(DB):
            cr[:NS, C_VSEL + h * DB + b] = (t // DS == b) * np.exp((DS - 1 - t % DS) * log_g[h]) * SCALE
    slope = 2.0 ** (-8.0 * np.arange(1, H + 1) / H)
    cc = np.zeros((P, N_CC))
    k = np.arange(2 * P) - P
    dist = i[:, None] - k[None, :]
    for h in range(H):
        cc[:, C_BIAS + h * 2 * P:C_BIAS + (h + 1) * 2 * P] = \
            np.where((dist >= 0) & (dist < WINDOW), -slope[h] * dist, NEG)
    rows = [(b, g, s) for b in range(DB) for g in range(2) for s in range(DS)]
    for half in range(2):
        for r, (b, g, s) in enumerate(rows):
            dist = s + WINDOW - np.arange(WINDOW)
            row = np.full(AKEYS, NEG)
            row[:WINDOW] = np.where(dist < WINDOW, -slope[2 * half + g] * dist, NEG)
            for j in range(s + 1):
                row[WINDOW + b * DS + j] = -slope[2 * half + g] * (s - j)
            cc[r, C_BIASS + half * AKEYS:C_BIASS + (half + 1) * AKEYS] = row
    return {"c_ident": np.eye(P, dtype=np.float32), "c_ret": cr.astype(np.float32), "c_att": cc.astype(np.float32)}


def laid_out(x):
    f = {k: np.asarray(v) for k, v in x.items()}
    base = {"qk0": 0, "v": 1024, "gA": 1536, "xb": 2048, "gB": 2560, "qC": 3072, "kC": 3584, "vC": 3840, "gC": 4096}
    w = f["w_in"][0]
    units = []
    for kind, i in UNITS:
        if kind == "qk":
            cols = [w[:, i * DH:(i + 1) * DH], w[:, GW + i * DH:GW + (i + 1) * DH]]
        elif kind == "kvC":
            cols = [w[:, base[n] + i * DH:base[n] + (i + 1) * DH] for n in ("kC", "vC")]
        else:
            cols = [w[:, base[kind] + i * UNIT:base[kind] + (i + 1) * UNIT]]
        unit = np.concatenate(cols, axis=1)
        units.append(unit.reshape(KD, P, UNIT).transpose(1, 0, 2).reshape(P, KD * UNIT))
    par = np.zeros((P, N_PAR), np.float32)

    def put(name, rows):
        par[:, PAR[name]:PAR[name] + rows.shape[0]] = rows.T

    put("ret_g", f["ret_norm_g"].reshape(H, P))
    put("conv_w", f["conv_w"].reshape(CONV * H, P))
    put("conv_b", f["conv_b"].reshape(H, P))
    put("b_r", f["b_rgate"].reshape(H, P))
    put("b_i", f["b_igate"].reshape(H, P))
    put("lam", f["lru_lambda"].reshape(H, P))
    par[:, PAR["sink"]:PAR["sink"] + H] = f["attn_sinks"]
    for half in range(2):
        for r in range(2 * NS):
            par[r, PAR["sink_s"] + half] = f["attn_sinks"][0, 2 * half + r // DS % 2]
    wg = np.zeros((P, 2, H, P), np.float32)
    for a, name in enumerate(("w_rgate", "w_igate")):
        blocks = f[name][0]
        for n in range(2 * H):
            r = slice(64 * (n % 2), 64 * (n % 2) + 64)
            wg[r, a, n // 2, r] = blocks[n]
    return {
        "x_prompt": f["x_prompt"].reshape(SEQ, D), "x_sample": f["x_sample"].reshape(NS, D),
        "w_units": np.stack(units), "w_out": f["w_out"][0], "norm_g": f["norm_g"].reshape(D), "params": par,
        "qk_gain": np.concatenate([f["q_norm_g"][0], f["k_norm_g"][0]]),
        "w_gates": wg.reshape(P, 2 * H * P), "state_conv": f["state_conv"].reshape(DB * 3, GW),
        "state_lru": f["state_lru"].reshape(DB, GW), "state_ret": f["state_ret"][0],
        "cache_k": f["cache_swa_k"][0], "cache_v": f["cache_swa_v"][0], **constants(),
    }


OUTS = {"y_prompt": (SEQ, D), "y_sample": (NS, D), "p_ret": (H, DH, DH), "p_lru": (1, GW), "p_conv": (3, GW),
        "p_k": (WINDOW, 2, DH), "p_v": (WINDOW, 2, DH), "s_ret": (DB, H, DH, DH), "s_lru": (DB, GW),
        "s_conv": (DB * 3, GW), "s_k": (DB, WINDOW, 2, DH), "s_v": (DB, WINDOW, 2, DH)}
SHAPES = [(1, SEQ, D), (DB, DS, D), (1, 1, H, DH, DH), (1, 1, GW), (1, 1, 3, GW), (1, 1, WINDOW, 2, DH),
          (1, 1, WINDOW, 2, DH), (1, DB, H, DH, DH), (1, DB, GW), (1, DB, 3, GW), (1, DB, WINDOW, 2, DH),
          (1, DB, WINDOW, 2, DH)]


def kernel(**inputs):
    import concourse.bacc as bacc
    from concourse.bass_utils import run_bass_kernel_spmd

    nc = bacc.Bacc("TRN2", target_bir_lowering=False, num_devices=1)
    arrays = {k: np.ascontiguousarray(v) for k, v in laid_out(inputs).items()}
    io = {k: nc.dram_tensor(k, v.shape, F32, kind="ExternalInput").ap() for k, v in arrays.items()}
    for name, shape in OUTS.items():
        io[name] = nc.dram_tensor(f"out_{name}", shape, F32, kind="ExternalOutput").ap()
    layer(nc, io)
    r = run_bass_kernel_spmd(nc, [arrays], core_ids=[0]).results[0]
    return tuple(r[f"out_{name}"].reshape(shape) for name, shape in zip(OUTS, SHAPES))
```

```python
from contextlib import ExitStack

import numpy as np

import concourse.bass as bass
from concourse import mybir

F32 = mybir.dt.float32
F32R = mybir.dt.float32r
ALU = mybir.AluOpType
ACT = mybir.ActivationFunctionType
AX = mybir.AxisListType

P = 128
D = 1024
SEQ = 1024
DB, DS = 8, 4
NS = DB * DS
TOK = SEQ + NS
NT = SEQ // P
KD = D // P
GW = 512
H = 4
DH = GW // H
KM = 3 * GW // P
W_IN = 9 * GW
PIECES = 4
UNIT = 256
NU = W_IN // UNIT
CH = TOK // 3
CONV = 4
WINDOW = 128
EPS = 1e-6
NEG = -1e30
SCALE = DH ** -0.5
LRU_C = 8.0
XS = 4
AKEYS = WINDOW + NS

UNITS = [("v", 0), ("qk", 0), ("v", 1), ("qk", 1), ("qk", 2), ("qk", 3), ("gB", 0), ("gB", 1),
         ("xb", 0), ("xb", 1), ("gC", 0), ("gC", 1), ("kvC", 0), ("qC", 0), ("kvC", 1), ("qC", 1),
         ("gA", 0), ("gA", 1)]
TOKEN_MAJOR = ("v", "kvC", "qC")


def n_groups(u):
    return NT + 1 if UNITS[u][0] in TOKEN_MAJOR else 6


FOLDS = [u for u in range(NU) if UNITS[u][0] in TOKEN_MAJOR]
FIRST_GROUP = [sum(n_groups(v) for v in range(u)) for u in range(NU + 1)]
GROUPS = [(u, j) for u in range(NU) for j in range(n_groups(u))]


def freed(u, j):
    kind, i = UNITS[u]
    if kind in ("kvC", "qC"):
        return "kn_set" if kind == "kvC" else "qn_set", 9 * i + j + 1
    return "act_freed", sum(UNITS[v][0] not in ("kvC", "qC") for v, _ in GROUPS[:FIRST_GROUP[u] + j + 1])


K_ORDER = [*range(H, KM), *range(H)]
M_ROWS = (slice(H, KM), slice(0, H))


def m_count(t, piece):
    return 1 + (2 * piece + t if t < 2 else 2 * t + piece)


PAR = {"ret_g": 0, "conv_w": 4, "conv_b": 20, "b_r": 24, "b_i": 28, "lam": 32, "sink": 36, "sink_s": 40}
N_PAR = 42
C_MASK, C_QDEC, C_KDEC, C_MASKS, C_QDECS, C_VSEL = 0, 512, 1024, 1028, 1156, 1284
N_CR = 1316
C_BIAS, C_BIASS = 0, 1024
N_CC = C_BIASS + 2 * AKEYS


def layer(nc, io):
    gammas = [float(1.0 - 2.0 ** (-5.0 - h)) for h in range(H)]
    with ExitStack() as ctx:
        def sb(name, shape, dt=F32, scope=ctx):
            return scope.enter_context(nc.sbuf_tensor(name, shape, dt))

        def sem(name):
            return ctx.enter_context(nc.semaphore(name))

        big = sb("big", [P, 25088], F32R)
        h_hi = big[:, 0:KD * TOK].rearrange("p (k n) -> p k n", k=KD)
        h_lo = big[:, KD * TOK:2 * KD * TOK].rearrange("p (k n) -> p k n", k=KD)
        w_base = 2 * KD * TOK
        wsz = KD * UNIT

        def w_part(slot, part):
            a = w_base + (2 * slot + part) * wsz
            return big[:, a:a + wsz]

        def wo_part(i, part):
            a = w_base + 2 * D * i if i < 2 else (i - 2) * 2 * D if i < KM - 2 else \
                w_base + 2 * wsz + (i - KM + 2) * 2 * D
            return big[:, a + part * D:a + (part + 1) * D]

        h_samp = sb("h_samp", [P, KD, 2 * NS], F32R)
        mixed = sb("mixed", [P, 3 * H, TOK])
        raw = sb("raw", [P, wsz])
        ident = sb("ident", [P, P])
        ones = sb("ones", [P, P])
        par = sb("par", [P, N_PAR])
        gain = sb("gain", [P, 2, DH])
        st_T = sb("st_T", [P, H, NS])
        tails = sb("tails", [P, H, 36])
        stat = sb("stat", [P, 64])
        neghalf = sb("neghalf", [P, NS])
        junk = sb("junk", [P, UNIT])
        sp_t = sb("sp_t", [P, 8, H])

        flat = mixed[:, 0:2 * H, :].rearrange("p a n -> p (a n)")
        x_in = [flat[:, i * D:(i + 1) * D] for i in range(XS)]
        g_row = flat[:, XS * D:(XS + 1) * D]
        x_sq = flat[:, (XS + 1) * D:(XS + 2) * D]
        qk = [mixed[:, 2 * H + 2 * (h % 2):2 * H + 2 * (h % 2) + 2, :] for h in range(H)]

        with ExitStack() as r:
            v_tok = sb("v_tok", [P, 2, NT + 1, UNIT], scope=r)
            cr = sb("cr", [P, N_CR], scope=r)
            s0 = sb("s0", [P, DB, DH], scope=r)
            v_sel = sb("v_sel", [NS, DB, DH], scope=r)
            sT = sb("sT", [P, 2, P], scope=r)
            k_dec = sb("k_dec", [P, 2, P], scope=r)
            q_dec = sb("q_dec", [P, 2, P], scope=r)
            o_nrm = sb("o_nrm", [P, 2, P], scope=r)
            S = sb("S", [P, 2, P], scope=r)
            o_sq = sb("o_sq", [P, P], scope=r)
            o_rs = sb("o_rs", [P, 2, NS], scope=r)
            st_rows = sb("st_rows", [NS, GW], scope=r)
        with ExitStack() as r:
            XW = 3 + SEQ + DB * 7
            xb = sb("xb", [P, 2, XW], scope=r)
            cv = sb("cv", [P, 2, TOK], scope=r)
            rgs = sb("rg", [P, 2, TOK], scope=r)
            igs = sb("ig", [P, 2, TOK], scope=r)
            aa = sb("aa", [P, TOK], scope=r)
            tt = sb("tt", [P, TOK], scope=r)
            wg = sb("wg", [P, 2, H, P], scope=r)
        with ExitStack() as r:
            kT = sb("kT", [P, 2, TOK], scope=r)
            v_c = sb("v_c", [P, 2, NT + 1, DH], scope=r)
            cc = sb("cc", [P, N_CC], scope=r)
            qn = sb("qn", [P, 2, 2 * DH], scope=r)
            kn = sb("kn", [P, 2, DH], scope=r)
            qT = sb("qT", [P, 2, 2 * P], scope=r)
            pr = sb("pr", [P, 2, 2, 2 * P], scope=r)
            pT = sb("pT", [P, 2, 4 * P], scope=r)
            cache = sb("cache", [P, DB, DH], scope=r)
            kcT = sb("kcT", [P, DB, P], scope=r)
            tail_rows = sb("tail_rows", [36, GW], scope=r)
        with ExitStack() as r:
            gate_tmp = sb("gate_tmp", [P, 2, CH], scope=r)
            m_parts = sb("m_parts", [P, 2, 2 * KM * P], F32R, scope=r)
            m_hi = m_parts[:, :, 0:KM * P].rearrange("p s (k n) -> p s k n", k=KM)
            m_lo = m_parts[:, :, KM * P:].rearrange("p s (k n) -> p s k n", k=KM)
            m_samp = m_parts[:, NT % 2, 0:KM * 2 * NS].rearrange("p (k n) -> p k n", k=KM)
            x_res = sb("x_res", [P, 2, D], scope=r)
            y_out = sb("y_out", [P, 2, D], scope=r)

        pb = [ctx.enter_context(nc.psum_tensor(f"proj{i}", [P, 512], F32)) for i in range(3)]
        bb = [ctx.enter_context(nc.psum_tensor(f"branch{i}", [P, 512], F32)) for i in range(5)]

        y_banks = [(bb[0], bb[1]), (bb[2], bb[3]), (pb[0], pb[1])]
        ys_banks = (bb[4], pb[2])
        wo_raw = [raw[:, 0:D], raw[:, D:2 * D], y_out[:, 0, :], y_out[:, 1, :]]

        names = """norm_in const_in cr_in wg_in cc_in x_tile0 x_tile1 x_tile2 x_tile3 raw_in s0_in kcache_in vcache_in
            x_again0 x_again1 wo_in0 wo_in1 wo_in2 wo_in3
            stored_cache stored_ret stored_tails stored_kv stored_y0 stored_y1
            ones_set x_ss x_pow x_scaled x_turned_a x_turned_b h_hi_set h_lo_set hs_hi_set hs_lo_set
            w_hi_set w_lo_set proj_done act_freed fold_set folded
            scores_done kturn_done masked kdec_set qdec_set vsel_set o_done kv_done kv2_done s_set s2_set
            o_ss o_pow o_ms o_root o_set oT_done mix_a
            st_turned st_copied lam_exp decay_set conv_set gates_done gates_read exp_set m2_set m_set
            lru_set xb_set tails_turned tails_copied
            k_ss k_pow kn_set kT_done kT_set q_ss q_pow qn_half qn_set qT_done qT_set
            sc_done biased mx_set ex_set pr_set pT_done pT_set av_done mix_c
            kc_turned kc_copied ssT_done ssT_part ssT_set ss_done smx_set sex_set spr_set spT_done
            spT_part spT_set sav_done smix_half smix_c
            mix_g m_hi_set m_lo_set y_done y_set ys_done ys_part ys_copied
            chain_v chain_a chain_p""".split()
        S_ = {n: sem(n) for n in names}

        def stat_col(i, n=1):
            return stat[:, i:i + n]

        block = ctx.enter_context(nc.Block())

        def tile_rows(t):
            return P if t < NT else NS

        def chunk_cols(c):
            return slice(c * P, c * P + tile_rows(c))

        n_stores = {}

        @block.sync
        def _(sp):
            def store(dst, src, name):
                sp.dma_start(dst, src).then_inc(S_[name], 16)
                n_stores[name] = n_stores.get(name, 0) + 16

            def load_w(u):
                if u > 0:
                    sp.wait_ge(S_["w_hi_set"], PIECES * u)
                    sp.wait_ge(S_["w_lo_set"], PIECES * u)
                sp.dma_start(raw[:], io["w_units"][u]).then_inc(S_["raw_in"], 16)

            def x_rows(t):
                return io["x_prompt"][t * P:(t + 1) * P, :] if t < NT else io["x_sample"]

            def load_x(t):
                if t >= XS:
                    sp.wait_ge(S_["x_turned_b"], t - XS + 1)
                sp.dma_start(x_in[t % XS][0:tile_rows(t), :], x_rows(t)).then_inc(S_[f"x_tile{t % XS}"], 16)

            load_x(0)
            sp.dma_start(g_row, io["norm_g"].partition_broadcast(P)).then_inc(S_["norm_in"], 16)
            sp.dma_start(ident[:], io["c_ident"]).then_inc(S_["norm_in"], 16)
            load_x(1)
            load_w(0)
            load_x(2)
            load_x(3)
            sp.dma_start(par[:], io["params"]).then_inc(S_["const_in"], 16)
            sp.dma_start(gain[:].rearrange("p a d -> p (a d)"), io["qk_gain"].partition_broadcast(P)).then_inc(
                S_["const_in"], 16)
            sp.dma_start(st_rows[0:24, :], io["state_conv"]).then_inc(S_["const_in"], 16)
            sp.dma_start(st_rows[24:32, :], io["state_lru"]).then_inc(S_["const_in"], 16)
            load_x(4)
            load_w(1)
            for t in range(5, NT + 1):
                load_x(t)
            sp.dma_start(cr[:], io["c_ret"]).then_inc(S_["cr_in"], 16)
            for hd in range(H):
                if hd > 0:
                    sp.wait_ge(S_["stored_ret"], 32 * hd)
                sp.dma_start(s0[:], io["state_ret"][:, hd].rearrange("b d e -> d b e")).then_inc(S_["s0_in"], 16)
                for u in ((2, 3, 4), (5, 6), (7,), (8,))[hd]:
                    load_w(u)
                if hd == 0:
                    for name, out in (("cache_k", "s_k"), ("cache_v", "s_v")):
                        store(io[out][:, 0:WINDOW - DS], io[name][:, DS:WINDOW], "stored_cache")
                sp.wait_ge(S_["s_set"], 9 * hd + 8)
                store(io["p_ret"][hd], S[:, hd % 2, :], "stored_ret")
                sp.wait_ge(S_["s2_set"], hd + 1)
                store(io["s_ret"][:, hd].rearrange("b d e -> d b e"), s0[:], "stored_ret")
            sp.wait_ge(S_["mix_a"], 36)
            sp.wait_ge(S_["stored_ret"], 32 * H)
            sp.dma_start(wg[:].rearrange("p a h n -> p (a h n)"), io["w_gates"]).then_inc(S_["wg_in"], 16)
            for u in range(9, 13):
                load_w(u)
            sp.wait_ge(S_["lru_set"], H)
            sp.dma_start(cc[:], io["c_att"]).then_inc(S_["cc_in"], 16)
            sp.dma_start(cache[:], io["cache_k"][:, :, 0].rearrange("b w d -> w b d")).then_inc(
                S_["kcache_in"], 16)
            load_w(13)
            load_w(14)
            sp.wait_ge(S_["tails_copied"], 1)
            store(io["s_conv"], tail_rows[0:24, :], "stored_tails")
            store(io["s_lru"], tail_rows[24:32, :], "stored_tails")
            store(io["p_conv"], tail_rows[32:35, :], "stored_tails")
            store(io["p_lru"], tail_rows[35:36, :], "stored_tails")
            for half in range(2):
                if half:
                    sp.wait_ge(S_["sav_done"], 1)
                    sp.dma_start(cache[:], io["cache_k"][:, :, 1].rearrange("b w d -> w b d")).then_inc(
                        S_["kcache_in"], 16)
                for t in (NT - 1, NT):
                    n9 = 9 * half + t
                    sp.wait_ge(S_["kn_set"], n9 + 1)
                    if t < NT:
                        store(io["p_k"][:, half], kn[:, n9 % 2, :], "stored_kv")
                        store(io["p_v"][:, half], v_c[:, half, t, :], "stored_kv")
                        continue
                    for b in range(DB):
                        rows = slice(b * DS, (b + 1) * DS)
                        store(io["s_k"][b, WINDOW - DS:WINDOW, half], kn[rows, n9 % 2, :], "stored_kv")
                        store(io["s_v"][b, WINDOW - DS:WINDOW, half], v_c[rows, half, t, :], "stored_kv")
                load_w(15 + 2 * half)
                sp.wait_ge(S_["kc_turned"], 2 * half + 2)
                sp.dma_start(cache[:], io["cache_v"][:, :, half].rearrange("b w d -> w b d")).then_inc(
                    S_["vcache_in"], 16)
                if half == 0:
                    load_w(16)
            sp.wait_ge(S_["w_hi_set"], PIECES * NU)
            sp.wait_ge(S_["w_lo_set"], PIECES * NU)
            for i, k in enumerate(K_ORDER):
                if i >= 4:
                    sp.wait_ge(S_["w_hi_set"], PIECES * NU + i - 3)
                    sp.wait_ge(S_["w_lo_set"], PIECES * NU + i - 3)
                if i == 2:
                    sp.wait_ge(S_["m_hi_set"], 1)
                sp.dma_start(wo_raw[i % 4], io["w_out"][k * P:(k + 1) * P, :]).then_inc(S_[f"wo_in{i % 4}"], 16)
                if i == 3:
                    for t in range(2):
                        sp.dma_start(x_res[:, t, :], x_rows(t)).then_inc(S_[f"x_again{t}"], 16)
            for t in range(NT + 1):
                sp.wait_ge(S_["y_set"], 2 * t + 2)
                if t < NT:
                    store(io["y_prompt"][t * P:(t + 1) * P, :], y_out[:, t % 2, :], f"stored_y{t % 2}")
                else:
                    store(io["y_sample"], y_out[0:NS, t % 2, :], f"stored_y{t % 2}")
                if t + 2 <= NT:
                    sp.dma_start(x_res[0:tile_rows(t + 2), t % 2, :], x_rows(t + 2)).then_inc(
                        S_[f"x_again{t % 2}"], 16)
            for name, n in n_stores.items():
                sp.wait_ge(S_[name], n)

        RET_UNIT = {2: 0, 4: 1, 5: 2, 6: 3}
        LRU_AT = {
            "conv": {(8, 6): 0, (9, 0): 1, (9, 6): 2, (10, 0): 3},
            "gates": {(8, 11): 0, (9, 6): 1, (10, 1): 2, (10, 9): 3},
            "m2": {(9, 2): 0, (9, 8): 1, (10, 3): 2, (10, 11): 3},
            "sqrt": {(9, 3): 0, (9, 9): 1, (10, 4): 2, (11, 0): 3},
            "scan": {(9, 4): 0, (9, 10): 1, (10, 5): 2, (11, 1): 3},
        }
        TAILS_AT = (12, 10)
        W_AT = (3, 5, 7, 9)

        def att_slot(u, s):
            if u in (13, 15):
                return (u - 13) // 2, s
            if u == 14:
                return 0, s + 18
            if u == 16:
                return 1, s + 18
            if u == 17 and s < 6:
                return 1, s + 30
            return None

        @block.tensor
        def _(pe):
            def three_pass(out, a_hi, a_lo, b_hi, b_lo, first, last):
                pe.matmul(out, a_lo, b_hi, start=first, stop=False)
                pe.matmul(out, a_hi, b_lo, start=False, stop=False)
                return pe.matmul(out, a_hi, b_hi, start=False, stop=last)

            def sample_pass(out, a, b_hi, b_lo, first, last):
                if first:
                    pe.matmul(out[0:2 * NS, :], a, b_hi, start=True, stop=False)
                mm = pe.matmul(out[0:NS, :], a[:, 0:NS], b_lo, start=False, stop=False)
                if not first:
                    mm = pe.matmul(out[0:2 * NS, :], a, b_hi, start=False, stop=last)
                return mm

            def group_half(u, j, half):
                g = FIRST_GROUP[u] + j
                bank = pb[g % 3]
                if half == 0:
                    if j == 0:
                        pe.wait_ge(S_["w_lo_set"], PIECES * (u + 1))
                        pe.wait_ge(S_["w_hi_set"], PIECES * (u + 1))
                    if g >= 3:
                        name, n = freed(*GROUPS[g - 3])
                        pe.wait_ge(S_[name], n)
                for k in range(4 * half, 4 * half + 4):
                    if UNITS[u][0] in TOKEN_MAJOR:
                        n = tile_rows(j)
                        cols = chunk_cols(j)
                        w = [w_part(u % 2, i)[:, k * UNIT:(k + 1) * UNIT] for i in range(2)]
                        if j == NT:
                            mm = sample_pass(bank[:, 0:UNIT], h_samp[:, k, :], w[0], w[1], k == 0, k == KD - 1)
                            continue
                        mm = three_pass(bank[0:n, 0:UNIT], h_hi[:, k, cols], h_lo[:, k, cols], w[0], w[1],
                                        k == 0, k == KD - 1)
                    else:
                        mt, c = j // 3, j % 3
                        cols = slice(c * CH, (c + 1) * CH)
                        w = [w_part(u % 2, i)[:, k * UNIT + mt * P:k * UNIT + (mt + 1) * P] for i in range(2)]
                        mm = three_pass(bank[:, 0:CH], w[0], w[1], h_hi[:, k, cols], h_lo[:, k, cols],
                                        k == 0, k == KD - 1)
                if half == 1:
                    mm.then_inc(S_["proj_done"], 1)

            def turn_x(t):
                n = tile_rows(t)
                pe.wait_ge(S_["x_scaled"], t + 1)
                for q in range(2):
                    bank = bb[2 * (t % 2) + q]
                    if t >= 2:
                        pe.wait_ge(S_["h_lo_set"], 2 * (t - 2) + q + 1)
                    for i in range(4):
                        k = 4 * q + i
                        mm = pe.transpose(bank[:, i * P:i * P + n], x_in[t % XS][0:n, k * P:(k + 1) * P],
                                          ident[0:n, 0:n])
                    mm.then_inc(S_["x_turned_b" if q else "x_turned_a"], 1)

            def ret_one(m):
                hd, c = divmod(m, 9)
                n, cols = tile_rows(c), chunk_cols(c)
                if c == 0:
                    pe.wait_ge(S_["act_freed"], freed(UNITS.index(("qk", hd)), 5)[1])
                if m == 0:
                    pe.wait_ge(S_["h_lo_set"], 2 * NT + 2)
                if m > 0:
                    pe.wait_ge(S_["masked"], m)
                pe.matmul(bb[0][0:n, 0:n], qk[hd][:, 1, cols], qk[hd][:, 0, cols], start=True,
                          stop=True).then_inc(S_["scores_done"], 1)
                if m > 0:
                    pe.wait_ge(S_["kdec_set"], m)
                pe.transpose(bb[1][0:n, 0:P], qk[hd][:, 1, cols], ident[:]).then_inc(S_["kturn_done"], 1)

            def ret_two(m):
                hd, c = divmod(m, 9)
                n = tile_rows(c)
                v = v_tok[0:n, hd // 2, c, (hd % 2) * DH:(hd % 2 + 1) * DH]
                if c == 0:
                    pe.wait_ge(S_["act_freed"], freed(UNITS.index(("v", hd // 2)), 8)[1])
                pe.wait_ge(S_["masked"], m + 1)
                pe.wait_ge(S_["qdec_set"], m + 1)
                if m > 0:
                    pe.wait_ge(S_["o_set"], m)
                o = bb[2]
                if c < NT:
                    mm = pe.matmul(o[:, 0:DH], sT[:, m % 2, :], v, start=True, stop=(c == 0))
                    if c > 0:
                        pe.wait_ge(S_["s_set"], m)
                        mm = pe.matmul(o[:, 0:DH], q_dec[:, m % 2, :], S[:, hd % 2, :], start=False, stop=True)
                else:
                    pe.wait_ge(S_["s0_in"], 16 * (hd + 1))
                    mm = pe.matmul(o[:, 0:NS], v, sT[0:n, m % 2, 0:n], start=True, stop=False,
                                   skip_group_check=True)
                    for b in range(DB):
                        cols = slice(b * DS, (b + 1) * DS)
                        mm = pe.matmul(o[:, cols], s0[:, b, :], q_dec[:, m % 2, cols], start=False,
                                       stop=(b == DB - 1), skip_group_check=True)
                mm.then_inc(S_["o_done"], 1)
                pe.wait_ge(S_["kdec_set"], m + 1)
                if m > 0:
                    pe.wait_ge(S_["s_set"], m)
                if c == 0 and hd > 0:
                    pe.wait_ge(S_["s2_set"], hd)
                if c < NT:
                    mm = pe.matmul(bb[3][:, 0:DH], k_dec[:, m % 2, :], v, start=True, stop=True)
                else:
                    pe.wait_ge(S_["vsel_set"], DB * (hd + 1))
                    mm = pe.matmul(bb[3][:, :], k_dec[0:n, m % 2, :],
                                   v_sel[:, 0:4, :].rearrange("p b d -> p (b d)"), start=True, stop=True)
                mm.then_inc(S_["kv_done"], 1)

            def ret_three(m):
                hd, c = divmod(m, 9)
                if c < NT:
                    pe.wait_ge(S_["o_set"], m + 1)
                    if m > 0:
                        pe.wait_ge(S_["mix_a"], m)
                    pe.transpose(bb[4][:, 0:P], o_nrm[:, m % 2, :], ident[:]).then_inc(S_["oT_done"], 1)
                else:
                    pe.wait_ge(S_["o_ss"], m + 1)
                    pe.wait_ge(S_["mix_a"], m)
                    pe.wait_ge(S_["ones_set"], 1)
                    pe.matmul(bb[4][:, 0:NS], ones[:], o_sq[:, 0:NS], start=True, stop=True).then_inc(
                        S_["oT_done"], 1)
                    pe.wait_ge(S_["s_set"], m + 1)
                    pe.matmul(bb[3][:, :], k_dec[0:NS, m % 2, :],
                              v_sel[:, 4:8, :].rearrange("p b d -> p (b d)"), start=True,
                              stop=True).then_inc(S_["kv2_done"], 1)

            def turn_states():
                pe.wait_ge(S_["const_in"], 64)
                for f in range(H):
                    mm = pe.transpose(bb[4][:, f * NS:(f + 1) * NS], st_rows[:, f * P:(f + 1) * P],
                                      ident[0:NS, 0:NS])
                mm.then_inc(S_["st_turned"], 1)

            GATE_BANKS = [0, 1, 2, 3, 4, 0]

            def lru_gates(f):
                pe.wait_ge(S_["conv_set"], f + 1)
                if f == 0:
                    pe.wait_ge(S_["wg_in"], 16)
                    pe.wait_ge(S_["mix_a"], 36)
                for q in range(6):
                    gate, c = divmod(q, 3)
                    if q == 5:
                        pe.wait_ge(S_["gates_read"], 6 * f + 1)
                    elif f > 0:
                        pe.wait_ge(S_["gates_read"], 6 * f)
                    pe.matmul(bb[GATE_BANKS[q]][:, 0:CH], wg[:, gate, f, :], cv[:, f % 2, c * CH:(c + 1) * CH],
                              start=True, stop=True).then_inc(S_["gates_done"], 1)

            def turn_tails():
                pe.wait_ge(S_["lru_set"], H)
                pe.wait_ge(S_["gates_read"], 24)
                for f in range(H):
                    mm = pe.transpose(bb[4][0:36, f * P:(f + 1) * P], tails[:, f, :], ident[:])
                mm.then_inc(S_["tails_turned"], 1)

            def turn_k(n9):
                t = n9 % 9
                n = tile_rows(t)
                pe.wait_ge(S_["kn_set"], n9 + 1)
                if n9 > 0:
                    pe.wait_ge(S_["kT_set"], n9)
                    if n9 >= 9:
                        pe.wait_ge(S_["qT_set"], 9)
                else:
                    pe.wait_ge(S_["gates_read"], 24)
                pe.transpose(bb[0][:, 0:n], kn[0:n, n9 % 2, :], ident[0:n, 0:n]).then_inc(S_["kT_done"], 1)

            def att_q(n9):
                t = n9 % 9
                n = tile_rows(t)
                pe.wait_ge(S_["qn_set"], n9 + 1)
                pe.wait_ge(S_["kT_set"], 9 * (n9 // 9) + 9)
                if n9 > 0:
                    pe.wait_ge(S_["qT_set"], n9)
                for g in range(2):
                    mm = pe.transpose(bb[0][:, g * n:(g + 1) * n], qn[0:n, n9 % 2, g * DH:(g + 1) * DH],
                                      ident[0:n, 0:n])
                mm.then_inc(S_["qT_done"], 1)

            def att_scores(half, t):
                n8 = 8 * half + t
                pe.wait_ge(S_["qT_set"], 9 * half + t + 1)
                if n8 > 0:
                    pe.wait_ge(S_["biased"], n8)
                for g in range(2):
                    lo = P if t == 0 else 0
                    mm = pe.matmul(bb[1][:, g * 2 * P + lo:(g + 1) * 2 * P],
                                   qT[:, (9 * half + t) % 2, g * P:(g + 1) * P],
                                   kT[:, half, (t - 1) * P + lo:(t + 1) * P], start=(g == 0), stop=True,
                                   skip_group_check=True)
                mm.then_inc(S_["sc_done"], 1)

            def att_turn(half, t):
                n8 = 8 * half + t
                pe.wait_ge(S_["pr_set"], n8 + 1)
                if n8 > 0:
                    pe.wait_ge(S_["pT_set"], n8)
                for kt in range(1 if t == 0 else 0, 2):
                    for g in range(2):
                        mm = pe.transpose(bb[2][:, (kt * 2 + g) * P:(kt * 2 + g + 1) * P],
                                          pr[:, n8 % 2, g, kt * P:(kt + 1) * P], ident[:])
                mm.then_inc(S_["pT_done"], 1)

            def att_values(half, t):
                n8 = 8 * half + t
                pe.wait_ge(S_["pT_set"], n8 + 1)
                if n8 > 0:
                    pe.wait_ge(S_["mix_c"], n8)
                for kt in range(1 if t == 0 else 0, 2):
                    mm = pe.matmul(bb[3][:, 0:2 * P], v_c[:, half, t - 1 + kt, :],
                                   pT[:, n8 % 2, kt * 2 * P:(kt + 1) * 2 * P], start=(kt == 0 or t == 0),
                                   stop=(kt == 1))
                mm.then_inc(S_["av_done"], 1)

            def cache_turn(half, q):
                pe.wait_ge(S_["kcache_in"], 16 * (half + 1))
                if half == 0 and q == 0:
                    pe.wait_ge(S_["tails_copied"], 1)
                if q == 1:
                    pe.wait_ge(S_["kc_copied"], 2 * half + 1)
                if half == 1 and q == 0:
                    pe.wait_ge(S_["smix_c"], 1)
                for i in range(4):
                    mm = pe.transpose(bb[4][:, i * P:(i + 1) * P], cache[:, 4 * q + i, :], ident[:])
                mm.then_inc(S_["kc_turned"], 1)

            def sample_q(half):
                return qT[:, (9 * half + NT) % 2, 0:2 * NS].rearrange("p (g b i) -> p b g i", g=2, b=DB)

            def samp_scores(half):
                pe.wait_ge(S_["qT_set"], 9 * half + 9)
                pe.wait_ge(S_["kc_copied"], 2 * half + 2)
                q = sample_q(half)
                for b in range(DB):
                    pe.matmul(bb[4][:, 8 * b:8 * b + 8], kcT[:, b, :], q[:, b], start=(b == 0), stop=True,
                              skip_group_check=True)
                mm = pe.matmul(bb[4][0:NS, 2 * NS:4 * NS], kT[:, half, SEQ:TOK], q, start=False, stop=True,
                               skip_group_check=True)
                mm.then_inc(S_["ssT_done"], 1)

            def samp_turn(half):
                pe.wait_ge(S_["ssT_set"], half + 1)
                pe.transpose(bb[4][0:64, 0:P], kcT[:, 0, 0:64], ident[:])
                pe.transpose(bb[4][0:64, P:P + NS], kcT[0:NS, 0, 64:128], ident[0:NS, 0:NS]).then_inc(
                    S_["ss_done"], 1)

            def samp_pturn(half):
                pe.wait_ge(S_["spr_set"], half + 1)
                ps = kcT[0:64, 2, :]
                pn = kcT[0:64, 3, 0:NS]
                pe.transpose(bb[4][:, 0:64], ps, ident[0:64, 0:64])
                pe.transpose(bb[4][0:NS, 64:128], pn, ident[0:64, 0:64]).then_inc(S_["spT_done"], 1)

            def samp_values(half):
                pe.wait_ge(S_["spT_set"], half + 1)
                pe.wait_ge(S_["vcache_in"], 16 * (half + 1))
                pe.matmul(bb[4][:, 0:64], v_c[0:NS, half, NT, :], kcT[0:NS, 4, 64:128], start=True, stop=False,
                          skip_group_check=True)
                for b in range(DB):
                    mm = pe.matmul(bb[4][:, 8 * b:8 * b + 8], cache[:, b, :], kcT[:, 4, 8 * b:8 * b + 8],
                                   start=False, stop=(b == DB - 1), skip_group_check=True)
                mm.then_inc(S_["sav_done"], 1)

            def att_side(half, s):
                if s % 2 == 1 and 0 <= (s - 3) // 2 <= NT and s >= 3:
                    att_q(9 * half + (s - 3) // 2)
                if s % 2 == 0 and 0 <= (s - 4) // 2 < NT:
                    att_scores(half, (s - 4) // 2)
                if s % 2 == 0 and 0 <= (s - 8) // 2 < NT:
                    att_turn(half, (s - 8) // 2)
                if s % 2 == 0 and 0 <= (s - 12) // 2 < NT:
                    att_values(half, (s - 12) // 2)
                if s in (18, 19):
                    cache_turn(half, s - 18)
                if s == 22:
                    samp_scores(half)
                if s == 24:
                    samp_turn(half)
                if s == 28:
                    samp_pturn(half)
                if s == 30:
                    samp_values(half)

            def side(u, s):
                if u in RET_UNIT and s < 12:
                    base = 9 * RET_UNIT[u]
                    if s >= 3:
                        ret_three(base + s - 3)
                    if 1 <= s < 10:
                        ret_two(base + s - 1)
                    if s < 9:
                        ret_one(base + s)
                if u == 1 and s == 2:
                    turn_states()
                if (u, s) in LRU_AT["gates"]:
                    lru_gates(LRU_AT["gates"][u, s])
                if (u, s) == TAILS_AT:
                    turn_tails()
                if att_slot(u, s):
                    att_side(*att_slot(u, s))
                if UNITS[u][0] == "kvC" and s % 2 == 1 and s >= 3:
                    turn_k(9 * UNITS[u][1] + (s - 3) // 2)
                if UNITS[u][0] == "qC" and s == 1:
                    turn_k(9 * UNITS[u][1] + NT)

            pe.wait_ge(S_["norm_in"], 32)
            turn_x(0)
            turn_x(1)
            for u in range(NU):
                for j in range(n_groups(u)):
                    if u == 0:
                        pe.wait_ge(S_["h_hi_set"], 2 * j + 2)
                        pe.wait_ge(S_["h_lo_set"], 2 * j + 2)
                        if j == NT:
                            pe.wait_ge(S_["hs_hi_set"], 2)
                            pe.wait_ge(S_["hs_lo_set"], 2)
                    for half in range(2):
                        group_half(u, j, half)
                        if u == 0 and half == 0 and j + 2 <= NT:
                            turn_x(j + 2)
                        side(u, 2 * j + half)

            def out_tile(t, i):
                k = K_ORDER[i]
                if i == 0 or k == 0:
                    pe.wait_ge(S_["m_lo_set"], m_count(t, int(k == 0)))
                    pe.wait_ge(S_["m_hi_set"], m_count(t, int(k == 0)))
                if i == 0 and t == 2:
                    name, c = freed(NU - 1, 5)
                    pe.wait_ge(S_[name], c)
                if i == 0 and t >= 3:
                    pe.wait_ge(S_["y_set"], 2 * t - 4)
                for q in range(2):
                    cols = slice(q * 512, (q + 1) * 512)
                    out = y_banks[t % 3][q][:, :]
                    if t == NT:
                        mm = pe.matmul(out[0:2 * NS, :], m_samp[:, k, :], wo_part(i, 0)[:, cols],
                                       start=(i == 0), stop=(i == KM - 1))
                    else:
                        mm = three_pass(out, m_hi[:, t % 2, k, :], m_lo[:, t % 2, k, :],
                                        wo_part(i, 0)[:, cols], wo_part(i, 1)[:, cols], i == 0, i == KM - 1)
                    if i == KM - 1:
                        mm.then_inc(S_["ys_done" if t == NT else "y_done"], 1)

            LEAD = KM - 3
            for i in range(KM):
                pe.wait_ge(S_["w_hi_set"], PIECES * NU + i + 1)
                pe.wait_ge(S_["w_lo_set"], PIECES * NU + i + 1)
                out_tile(0, i)
                if i < LEAD:
                    out_tile(1, i)
            for i in range(LEAD, KM):
                out_tile(1, i)
            for t in range(2, NT + 1):
                for i in range(KM):
                    out_tile(t, i)
            for i in range(KM):
                for q in range(2):
                    mm = pe.matmul(ys_banks[q][0:NS, :], m_samp[:, K_ORDER[i], 0:NS],
                                   wo_part(i, 1)[:, q * 512:(q + 1) * 512], start=(i == 0), stop=(i == KM - 1))
                    if i == KM - 1:
                        mm.then_inc(S_["y_done"], 1)

        @block.scalar
        def _(act):
            def w_hi(u, piece):
                act.wait_ge(S_["raw_in"], 16 * (u + 1))
                if u >= 2:
                    act.wait_ge(S_["proj_done"], FIRST_GROUP[u - 1])
                cols = slice(piece * wsz // PIECES, (piece + 1) * wsz // PIECES)
                act.activation(w_part(u % 2, 0)[:, cols], raw[:, cols], ACT.Copy).then_inc(S_["w_hi_set"], 1)

            def x_stat(t):
                n = tile_rows(t)
                act.wait_ge(S_[f"x_tile{t % XS}"], 16 * (t // XS + 1))
                if t > 0:
                    act.wait_ge(S_["x_ss"], t)
                act.activation(x_sq[0:n, :], x_in[t % XS][0:n, :], ACT.Square,
                               accum_out=stat[0:n, t % XS:t % XS + 1]).then_inc(S_["x_ss"], 1)

            def x_hi(t):
                n = tile_rows(t)
                for q in range(2):
                    act.wait_ge(S_["x_turned_b" if q else "x_turned_a"], t + 1)
                    act.activation(h_hi[:, 4 * q:4 * q + 4, chunk_cols(t)],
                                   bb[2 * (t % 2) + q][:, :].rearrange("p (k n) -> p k n", k=4)[:, :, 0:n],
                                   ACT.Copy).then_inc(S_["h_hi_set"], 1)
                    if t == NT:
                        act.activation(h_samp[:, 4 * q:4 * q + 4, 0:NS],
                                       bb[2 * (t % 2) + q][:, :].rearrange("p (k n) -> p k n", k=4)[:, :, 0:n],
                                       ACT.Copy).then_inc(S_["hs_hi_set"], 1)

            def fold_copy(u):
                g, f = FIRST_GROUP[u] + NT, FOLDS.index(u)
                act.wait_ge(S_["proj_done"], g + 1)
                if UNITS[u][0] == "kvC":
                    act.wait_ge(S_["k_ss"], 2 * (9 * UNITS[u][1] + NT))
                if UNITS[u][0] == "qC":
                    act.wait_ge(S_["q_ss"], 2 * (9 * UNITS[u][1] + NT))
                act.activation(junk[0:NS, :], pb[g % 3][NS:2 * NS, 0:UNIT], ACT.Copy).then_inc(S_["fold_set"], 1)
                act.wait_ge(S_["folded"], f + 1)

            def evacuate(u, j):
                kind, i = UNITS[u]
                g = FIRST_GROUP[u] + j
                act.wait_ge(S_["proj_done"], g + 1)
                bank = pb[g % 3]
                mt, c = j // 3, j % 3
                cols = slice(c * CH, (c + 1) * CH)
                if kind == "v":
                    n = tile_rows(j)
                    ins = act.activation(v_tok[0:n, i, j, :], bank[0:n, 0:UNIT], ACT.Copy)
                elif kind == "qk":
                    if j == 0 and i >= 2:
                        act.wait_ge(S_["mix_a"], 9 * (i - 1))
                    ins = act.activation(qk[i][:, mt, cols], bank[:, 0:CH], ACT.Copy)
                elif kind in ("gB", "gC"):
                    if kind == "gC" and i == 0 and j == 0:
                        act.wait_ge(S_["mix_a"], 36)
                    row = (4 if kind == "gB" else 8) + 2 * i + mt
                    ins = act.activation(mixed[:, row, cols], bank[:, 0:CH], ACT.Silu)
                elif kind == "gA":
                    e = 6 * i + j
                    if e == 0:
                        act.wait_ge(S_["smix_c"], 1)
                    if e >= 2:
                        act.wait_ge(S_["mix_g"], e - 1)
                    ins = act.activation(gate_tmp[:, e % 2, :], bank[:, 0:CH], ACT.Silu)
                elif kind == "xb":
                    f = 2 * i + mt
                    if f >= 2:
                        act.wait_ge(S_["conv_set"], f - 1)
                    if f == 0 and j == 0:
                        act.wait_ge(S_["mix_a"], 36)
                        act.wait_ge(S_["stored_ret"], 32 * H)
                    n = min(CH, SEQ - c * CH)
                    if c == 2:
                        act.activation(xb[:, f % 2, 3 + SEQ:].rearrange("p (b i) -> p b i", b=DB)[:, :, 3:7],
                                       bank[:, n:CH].rearrange("p (b i) -> p b i", b=DB), ACT.Copy).then_inc(
                                           S_["xb_set"], 1)
                    ins = act.activation(xb[:, f % 2, 3 + c * CH:3 + c * CH + n], bank[:, 0:n], ACT.Copy)
                ins.then_inc(S_["act_freed"], 1)

            def ret_norm(m):
                hd, c = divmod(m, 9)
                act.wait_ge(S_["o_done"], m + 1)
                if c == 0 and hd > 0:
                    act.wait_ge(S_["oT_done"], m)
                if c < NT:
                    act.activation(o_sq[:, 0:P], bb[2][:, 0:P], ACT.Square,
                                   accum_out=stat[:, 4 + m % 2:5 + m % 2]).then_inc(S_["o_ss"], 1)
                    act.wait_ge(S_["o_pow"], 8 * hd + c + 1)
                    if m >= 2:
                        act.wait_ge(S_["mix_a"], m - 1)
                    act.activation(o_nrm[:, m % 2, :], bb[2][:, 0:P], ACT.Copy,
                                   scale=stat[:, 8 + m % 2:9 + m % 2]).then_inc(S_["o_set"], 1)
                else:
                    act.activation(o_sq[:, 0:NS], bb[2][:, 0:NS], ACT.Square).then_inc(S_["o_ss"], 1)
                    act.wait_ge(S_["mix_a"], m - 1)
                    act.activation(o_nrm[:, m % 2, 0:NS], bb[2][:, 0:NS], ACT.Copy).then_inc(S_["o_set"], 1)

            def lru_sig(f):
                dst = (rgs[:, f % 2, :], igs[:, f % 2, :])
                for q in range(6):
                    gate, c = divmod(q, 3)
                    if q == 0 and f >= 2:
                        act.wait_ge(S_["lru_set"], f - 1)
                    act.wait_ge(S_["gates_done"], 6 * f + q + 1)
                    col = PAR["b_r" if gate == 0 else "b_i"] + f
                    act.activation(dst[gate][:, c * CH:(c + 1) * CH], bb[[0, 1, 2, 3, 4, 0][q]][:, 0:CH],
                                   ACT.Sigmoid, bias=par[:, col:col + 1]).then_inc(S_["gates_read"], 1)
                act.wait_ge(S_["gates_read"], 6 * f + 6)
                if f == 0:
                    act.wait_ge(S_["decay_set"], 1)
                else:
                    act.wait_ge(S_["lru_set"], f)
                rg = rgs[:, f % 2, :]
                act.activation(aa[:], rg, ACT.Exp, scale=sp_t[:, 6, f:f + 1]).then_inc(S_["exp_set"], 1)
                act.activation(tt[:], rg, ACT.Tanh, scale=sp_t[:, 7, f:f + 1]).then_inc(S_["exp_set"], 1)

            def lru_sqrt(f):
                act.wait_ge(S_["m2_set"], f + 1)
                act.activation(rgs[:, f % 2, :], tt[:], ACT.Sqrt).then_inc(S_["m_set"], 1)

            def k_stat(u, j):
                half = UNITS[u][1]
                n = tile_rows(j)
                g, n9 = FIRST_GROUP[u] + j, 9 * half + j
                act.wait_ge(S_["proj_done"], g + 1)
                if u == 12 and j == 0:
                    act.wait_ge(S_["lru_set"], H)
                if n9 > 0:
                    act.wait_ge(S_["k_ss"], 2 * n9)
                if half == 1:
                    act.wait_ge(S_["q_ss"], 2 * (NT + 1))
                bank = pb[g % 3]
                act.activation(junk[0:n, 0:DH], bank[0:n, 0:DH], ACT.Square,
                               accum_out=stat[0:n, 12 + n9 % 2:13 + n9 % 2]).then_inc(S_["k_ss"], 1)
                act.activation(v_c[0:n, half, j, :], bank[0:n, DH:2 * DH], ACT.Copy).then_inc(S_["k_ss"], 1)

            def k_copy(n9):
                half, t = divmod(n9, 9)
                n = tile_rows(t)
                act.wait_ge(S_["kT_done"], n9 + 1)
                act.activation(kT[:, half, chunk_cols(t)], bb[0][:, 0:n], ACT.Copy).then_inc(S_["kT_set"], 1)

            def q_stat(u, j):
                half = UNITS[u][1]
                n = tile_rows(j)
                g, n9 = FIRST_GROUP[u] + j, 9 * half + j
                act.wait_ge(S_["proj_done"], g + 1)
                act.wait_ge(S_["k_ss"], 2 * (NT + 1) * (half + 1))
                if n9 > 0:
                    act.wait_ge(S_["q_ss"], 2 * n9)
                for i in range(2):
                    act.activation(junk[0:n, i * DH:(i + 1) * DH], pb[g % 3][0:n, i * DH:(i + 1) * DH], ACT.Square,
                                   accum_out=stat[0:n, 20 + 2 * (n9 % 2) + i:21 + 2 * (n9 % 2) + i]).then_inc(
                                       S_["q_ss"], 1)

            def q_copy(n9):
                n = tile_rows(n9 % 9)
                act.wait_ge(S_["qT_done"], n9 + 1)
                if n9 >= 2:
                    h2, t2 = divmod(n9 - 2, 9)
                    if t2 < NT:
                        act.wait_ge(S_["sc_done"], 8 * h2 + t2 + 1)
                    else:
                        act.wait_ge(S_["ssT_done"], h2 + 1)
                act.activation(qT[:, n9 % 2, 0:2 * n], bb[0][:, 0:2 * n], ACT.Copy).then_inc(S_["qT_set"], 1)

            def att_exp(half, t):
                n8 = 8 * half + t
                act.wait_ge(S_["mx_set"], n8 + 1)
                lo = P if t == 0 else 0
                c = 32 + 8 * (n8 % 2)
                for g in range(2):
                    act.activation(pr[:, n8 % 2, g, lo:], pr[:, n8 % 2, g, lo:], ACT.Exp,
                                   bias=stat[:, c + g:c + g + 1],
                                   accum_out=stat[:, c + 4 + g:c + 5 + g]).then_inc(S_["ex_set"], 1)
                act.activation(stat[:, c + 2:c + 4], stat[:, c + 2:c + 4], ACT.Exp).then_inc(S_["ex_set"], 1)

            def att_pcopy(half, t):
                n8 = 8 * half + t
                act.wait_ge(S_["pT_done"], n8 + 1)
                if n8 >= 2:
                    act.wait_ge(S_["av_done"], n8 - 1)
                lo = 2 * P if t == 0 else 0
                act.activation(pT[:, n8 % 2, lo:], bb[2][:, lo:], ACT.Copy).then_inc(S_["pT_set"], 1)

            def cache_copy(half, q):
                act.wait_ge(S_["kc_turned"], 2 * half + q + 1)
                act.activation(kcT[:, 4 * q:4 * q + 4, :], bb[4][:, :].rearrange("p (b n) -> p b n", b=4),
                               ACT.Copy).then_inc(S_["kc_copied"], 1)

            def samp_copy(half):
                act.wait_ge(S_["ssT_done"], half + 1)
                act.activation(kcT[:, 0, 0:64], bb[4][:, 0:64], ACT.Copy).then_inc(S_["ssT_part"], 1)
                act.activation(kcT[0:NS, 0, 64:128], bb[4][0:NS, 64:128], ACT.Copy).then_inc(S_["ssT_set"], 1)

            def samp_exp(half):
                act.wait_ge(S_["smx_set"], half + 1)
                act.activation(kcT[0:64, 2:4, :].rearrange("p a n -> p (a n)")[:, 0:AKEYS],
                               kcT[0:64, 5:7, :].rearrange("p a n -> p (a n)")[:, 0:AKEYS], ACT.Exp,
                               bias=stat[0:64, 48:49], accum_out=stat[0:64, 50:51]).then_inc(S_["sex_set"], 1)
                act.activation(stat[0:64, 49:50], stat[0:64, 49:50], ACT.Exp).then_inc(S_["sex_set"], 1)

            def samp_pcopy(half):
                act.wait_ge(S_["spT_done"], half + 1)
                act.activation(kcT[:, 4, 0:64], bb[4][:, 0:64], ACT.Copy).then_inc(S_["spT_part"], 1)
                act.activation(kcT[0:NS, 4, 64:128], bb[4][0:NS, 64:128], ACT.Copy).then_inc(S_["spT_set"], 1)

            def att_side(half, s):
                if s % 2 == 1 and 0 <= (s - 9) // 2 < NT:
                    att_pcopy(half, (s - 9) // 2)
                if s % 2 == 1 and s >= 3 and (s - 3) // 2 <= NT:
                    q_copy(9 * half + (s - 3) // 2)
                if s % 2 == 1 and 0 <= (s - 5) // 2 < NT:
                    att_exp(half, (s - 5) // 2)
                if s in (18, 19):
                    cache_copy(half, s - 18)
                if s == 23:
                    samp_copy(half)
                if s == 26:
                    samp_exp(half)
                if s == 29:
                    samp_pcopy(half)

            def side(u, s):
                if s in W_AT and u + 1 < NU:
                    w_hi(u + 1, W_AT.index(s))
                if (u, s) == (1, 4):
                    lam_exp()
                if (u, s) in ((17, 6), (17, 8)):
                    wo_high((s - 6) // 2)
                if (u, s) in ((17, 3), (17, 4)):
                    m_high(s - 3, 0)
                if (u, s) == (17, 10):
                    m_high(0, 1)
                    m_high(1, 1)
                if u in RET_UNIT and 1 <= s < 10:
                    ret_norm(9 * RET_UNIT[u] + s - 1)
                if u in RET_UNIT and s == 11:
                    act.wait_ge(S_["o_ms"], RET_UNIT[u] + 1)
                    act.activation(o_rs[:, 1, :], o_rs[:, 0, :], ACT.Sqrt).then_inc(S_["o_root"], 1)
                if (u, s) in LRU_AT["gates"]:
                    lru_sig(LRU_AT["gates"][u, s])
                if (u, s) in LRU_AT["sqrt"]:
                    lru_sqrt(LRU_AT["sqrt"][u, s])
                if UNITS[u][0] == "kvC" and s % 2 == 1 and s >= 3:
                    k_copy(9 * UNITS[u][1] + (s - 3) // 2)
                if UNITS[u][0] == "qC" and s == 1:
                    k_copy(9 * UNITS[u][1] + NT)
                if att_slot(u, s):
                    att_side(*att_slot(u, s))
                if (u, s) == (TAILS_AT[0], TAILS_AT[1] + 1):
                    act.wait_ge(S_["tails_turned"], 1)
                    act.activation(tail_rows[:], bb[4][0:36, :], ACT.Copy).then_inc(S_["tails_copied"], 1)

            def wo_high(i):
                act.wait_ge(S_[f"wo_in{i % 4}"], 16 * (i // 4 + 1))
                act.wait_ge(S_["proj_done"], FIRST_GROUP[NU - 1 if i < 2 else NU])
                act.activation(wo_part(i, 0), wo_raw[i % 4], ACT.Copy).then_inc(S_["w_hi_set"], 1)

            def m_high(t, piece):
                n = tile_rows(t)
                if t == 0 and piece == 0:
                    act.wait_ge(S_["smix_c"], 2)
                    act.wait_ge(S_["mix_c"], 16)
                    act.wait_ge(S_["stored_kv"], n_stores["stored_kv"])
                last = min(SEQ if t < NT else TOK, (t + 1) * P)
                if piece == 1:
                    act.wait_ge(S_["mix_g"], 9 + -(-last // CH))
                if t >= 2:
                    act.wait_ge(S_["y_done"], 2 * (t - 1))
                rows = M_ROWS[piece]
                hi = m_hi[:, t % 2, rows, :] if t < NT else m_samp[:, rows, 0:NS]
                act.activation(hi, mixed[:, rows, chunk_cols(t)], ACT.Copy).then_inc(
                    S_["m_hi_set"], 1)

            def lam_exp():
                act.wait_ge(S_["const_in"], 64)
                act.activation(sp_t[:, 0, :], par[:, PAR["lam"]:PAR["lam"] + H], ACT.Abs).then_inc(
                    S_["chain_a"], 1)
                act.wait_ge(S_["chain_a"], 1)
                act.activation(sp_t[:, 1, :], sp_t[:, 0, :], ACT.Exp, scale=-1.0).then_inc(S_["lam_exp"], 1)

            x_stat(0)
            x_stat(1)
            x_hi(0)
            for i in range(PIECES):
                w_hi(0, i)
            x_stat(2)
            x_hi(1)
            for u in range(NU):
                for j in range(n_groups(u)):
                    if u == 0:
                        if j + 3 <= NT:
                            x_stat(j + 3)
                        if j + 2 <= NT:
                            x_hi(j + 2)
                    side(u, 2 * j)
                    if j == NT:
                        fold_copy(u)
                    if UNITS[u][0] == "kvC":
                        k_stat(u, j)
                    elif UNITS[u][0] == "qC":
                        q_stat(u, j)
                    else:
                        evacuate(u, j)
                    side(u, 2 * j + 1)

            for i in range(2, KM):
                wo_high(i)
            for t in range(2, NT + 1):
                for piece in range(2):
                    m_high(t, piece)
            act.wait_ge(S_["stored_y1"], 16 * (NT // 2))
            act.wait_ge(S_["ys_done"], 2)
            for q in range(2):
                act.activation(y_out[0:NS, 1, q * 512:(q + 1) * 512], y_banks[NT % 3][q][NS:2 * NS, :],
                               ACT.Copy).then_inc(S_["ys_copied"], 1)

        @block.vector
        def _(dve):
            count = [0]

            def link(ins):
                count[0] += 1
                ins.then_inc(S_["chain_v"], 1)
                dve.wait_ge(S_["chain_v"], count[0])

            def w_low(u, piece):
                dve.wait_ge(S_["w_hi_set"], PIECES * u + piece + 1)
                cols = slice(piece * wsz // PIECES, (piece + 1) * wsz // PIECES)
                dve.tensor_tensor(w_part(u % 2, 1)[:, cols], raw[:, cols], w_part(u % 2, 0)[:, cols].bitcast(F32),
                                  ALU.subtract).then_inc(S_["w_lo_set"], 1)

            def x_scale(t):
                n = tile_rows(t)
                dve.wait_ge(S_["x_pow"], t + 1)
                if t == 0:
                    dve.wait_ge(S_["norm_in"], 32)
                dve.scalar_tensor_tensor(out=x_in[t % XS][0:n, :], in0=x_in[t % XS][0:n, :],
                                         scalar=stat[0:n, 52 + t % XS:53 + t % XS], in1=g_row[0:n, :],
                                         op0=ALU.mult, op1=ALU.mult).then_inc(S_["x_scaled"], 1)

            def x_lo(t):
                n = tile_rows(t)
                for q in range(2):
                    dve.wait_ge(S_["h_hi_set"], 2 * t + q + 1)
                    if t == NT:
                        dve.wait_ge(S_["hs_hi_set"], q + 1)
                    dve.tensor_tensor(h_lo[:, 4 * q:4 * q + 4, chunk_cols(t)],
                                      bb[2 * (t % 2) + q][:, :].rearrange("p (k n) -> p k n", k=4)[:, :, 0:n],
                                      h_hi[:, 4 * q:4 * q + 4, chunk_cols(t)].bitcast(F32),
                                      ALU.subtract).then_inc(S_["h_lo_set"], 1)
                    if t == NT:
                        dve.tensor_tensor(h_samp[:, 4 * q:4 * q + 4, NS:],
                                          bb[2 * (t % 2) + q][:, :].rearrange("p (k n) -> p k n", k=4)[:, :, 0:n],
                                          h_samp[:, 4 * q:4 * q + 4, 0:NS].bitcast(F32),
                                          ALU.subtract).then_inc(S_["hs_lo_set"], 1)

            def ret_mask(m):
                hd, c = divmod(m, 9)
                n = tile_rows(c)
                dve.wait_ge(S_["scores_done"], m + 1)
                if m == 0:
                    dve.wait_ge(S_["cr_in"], 16)
                if m >= 2:
                    dve.wait_ge(S_["o_done"], m - 1)
                mask = cr[:, C_MASK + hd * P:C_MASK + (hd + 1) * P] if c < NT else \
                    cr[0:NS, C_MASKS + hd * NS:C_MASKS + (hd + 1) * NS]
                dve.tensor_tensor(sT[0:n, m % 2, 0:n], bb[0][0:n, 0:n], mask, ALU.mult).then_inc(S_["masked"], 1)
                dve.wait_ge(S_["kturn_done"], m + 1)
                if m >= 2:
                    dve.wait_ge(S_["kv_done"], m - 1)
                if c < NT:
                    ins = dve.tensor_scalar(k_dec[:, m % 2, :], bb[1][:, 0:P],
                                            cr[:, C_KDEC + hd:C_KDEC + hd + 1], None, ALU.mult)
                else:
                    ins = dve.tensor_copy(k_dec[0:n, m % 2, :], bb[1][0:n, 0:P])
                ins.then_inc(S_["kdec_set"], 1)

            def ret_state(m):
                hd, c = divmod(m, 9)
                dve.wait_ge(S_["kv_done"], m + 1)
                dve.wait_ge(S_["o_done"], m + 1)
                if c == 0:
                    if hd >= 2:
                        dve.wait_ge(S_["stored_ret"], 32 * (hd - 1))
                    ins = dve.tensor_copy(S[:, hd % 2, :], bb[3][:, 0:DH])
                elif c < NT:
                    ins = dve.scalar_tensor_tensor(out=S[:, hd % 2, :], in0=S[:, hd % 2, :],
                                                   scalar=float(gammas[hd] ** P), in1=bb[3][:, 0:DH],
                                                   op0=ALU.mult, op1=ALU.add)
                else:
                    ins = samp_state(hd, 0)
                ins.then_inc(S_["s_set"], 1)

            def samp_state(hd, q):
                part = s0[:, 4 * q:4 * q + 4, :].rearrange("p b e -> p (b e)")
                return dve.scalar_tensor_tensor(out=part, in0=part, scalar=float(gammas[hd] ** DS),
                                                in1=bb[3][:, :], op0=ALU.mult, op1=ALU.add)

            def ret_mix(m):
                hd, c = divmod(m, 9)
                dve.wait_ge(S_["oT_done"], m + 1)
                g = par[:, PAR["ret_g"] + hd:PAR["ret_g"] + hd + 1]
                if c < NT:
                    dve.tensor_scalar(mixed[:, hd, chunk_cols(c)], bb[4][:, 0:P], g, None, ALU.mult).then_inc(
                        S_["mix_a"], 1)
                else:
                    link(dve.tensor_scalar(o_rs[:, 0, :], bb[4][:, 0:NS], 1.0 / DH, EPS, ALU.mult, ALU.add))
                    dve.reciprocal(o_rs[:, 0, :], o_rs[:, 0, :]).then_inc(S_["o_ms"], 1)
                    dve.wait_ge(S_["kv2_done"], hd + 1)
                    samp_state(hd, 1).then_inc(S_["s2_set"], 1)
                    dve.wait_ge(S_["o_set"], m + 1)
                    dve.wait_ge(S_["o_root"], hd + 1)
                    dve.scalar_tensor_tensor(out=mixed[:, hd, SEQ:TOK], in0=o_nrm[:, m % 2, 0:NS], scalar=g,
                                             in1=o_rs[:, 1, :], op0=ALU.mult, op1=ALU.mult).then_inc(
                                                 S_["mix_a"], 1)

            def softplus():
                lam = par[:, PAR["lam"]:PAR["lam"] + H]
                a, y, s, s2, acc, relu = (sp_t[:, i, :] for i in range(6))
                dve.wait_ge(S_["lam_exp"], 1)
                link(dve.tensor_scalar(a, y, 2.0, None, ALU.add))
                link(dve.reciprocal(a, a))
                link(dve.tensor_tensor(s, y, a, ALU.mult))
                link(dve.tensor_tensor(s2, s, s, ALU.mult))
                link(dve.tensor_scalar(acc, s2, 2.0 / 19, 2.0 / 17, ALU.mult, ALU.add))
                for d in (15, 13, 11, 9, 7, 5, 3, 1):
                    link(dve.tensor_tensor(acc, acc, s2, ALU.mult))
                    link(dve.tensor_scalar(acc, acc, 2.0 / d, None, ALU.add))
                link(dve.tensor_tensor(acc, acc, s, ALU.mult))
                link(dve.tensor_scalar(relu, lam, -1.0, 0.0, ALU.mult, ALU.max))
                link(dve.tensor_tensor(acc, acc, relu, ALU.add))
                link(dve.tensor_scalar(sp_t[:, 6, :], acc, -LRU_C, None, ALU.mult))
                dve.tensor_scalar(sp_t[:, 7, :], acc, LRU_C, None, ALU.mult).then_inc(S_["decay_set"], 1)

            def conv(f):
                i = f % 2
                samp = xb[:, i, 3 + SEQ:].rearrange("p (b i) -> p b i", b=DB)
                if f == 0:
                    dve.wait_ge(S_["stored_ret"], 32 * H)
                if f < 2:
                    link(dve.memset(xb[:, i, 0:3], 0.0))
                link(dve.tensor_copy(samp[:, :, 0:3], st_T[:, f, 0:24].rearrange("p (b i) -> p b i", b=DB)))
                dve.wait_ge(S_["act_freed"], freed(8 + f // 2, 3 * (f % 2) + 2)[1])
                dve.wait_ge(S_["xb_set"], f + 1)
                w = [par[:, PAR["conv_w"] + 4 * j + f:PAR["conv_w"] + 4 * j + f + 1] for j in range(CONV)]
                b = par[:, PAR["conv_b"] + f:PAR["conv_b"] + f + 1]
                out_p = cv[:, i, 0:SEQ]
                out_s = cv[:, i, SEQ:TOK].rearrange("p (b i) -> p b i", b=DB)
                dve.tensor_scalar(out_p, xb[:, i, 0:SEQ], w[0], b, ALU.mult, ALU.add)
                link(dve.tensor_scalar(out_s, samp[:, :, 0:DS], w[0], b, ALU.mult, ALU.add))
                for j in range(1, CONV):
                    dve.scalar_tensor_tensor(out=out_p, in0=xb[:, i, j:j + SEQ], scalar=w[j], in1=out_p,
                                             op0=ALU.mult, op1=ALU.add)
                    last = dve.scalar_tensor_tensor(out=out_s, in0=samp[:, :, j:j + DS], scalar=w[j], in1=out_s,
                                                    op0=ALU.mult, op1=ALU.add)
                    if j < CONV - 1:
                        link(last)
                link(last)
                dve.tensor_copy(tails[:, f, 0:24].rearrange("p (b i) -> p b i", b=DB), samp[:, :, 4:7])
                dve.tensor_copy(tails[:, f, 32:35], xb[:, i, SEQ:SEQ + 3]).then_inc(S_["conv_set"], 1)

            def lru_m2(f):
                dve.wait_ge(S_["exp_set"], 2 * f + 2)
                dve.wait_ge(S_["gates_read"], 6 * f + 6)
                ig, rg, u = igs[:, f % 2, :], rgs[:, f % 2, :], cv[:, f % 2, :]
                dve.tensor_tensor(rg, aa[:], aa[:], ALU.mult)
                link(dve.tensor_tensor(u, ig, u, ALU.mult))
                dve.scalar_tensor_tensor(out=tt[:], in0=rg, scalar=1.0, in1=tt[:], op0=ALU.add,
                                         op1=ALU.mult).then_inc(S_["m2_set"], 1)

            def lru_scan(f):
                a_first = aa[:, SEQ:TOK].rearrange("p (b i) -> p b i", b=DB)[:, :, 0]
                u, rg, ig = cv[:, f % 2, :], rgs[:, f % 2, :], igs[:, f % 2, :]
                u_first = u[:, SEQ:TOK].rearrange("p (b i) -> p b i", b=DB)[:, :, 0]
                dve.wait_ge(S_["m_set"], f + 1)
                link(dve.memset(rg[:, 0:1], 1.0))
                link(dve.tensor_tensor(u, u, rg, ALU.mult))
                link(dve.tensor_tensor(ig[:, 0:DB], a_first, st_T[:, f, 24:32], ALU.mult))
                link(dve.tensor_tensor(u_first, u_first, ig[:, 0:DB], ALU.add))
                link(dve.memset(a_first, 0.0))
                link(dve.tensor_tensor_scan(tt[:], aa[:], u, 0.0, ALU.mult, ALU.add))
                dve.tensor_copy(tails[:, f, 24:32],
                                tt[:, SEQ:TOK].rearrange("p (b i) -> p b i", b=DB)[:, :, DS - 1])
                dve.tensor_copy(tails[:, f, 35:36], tt[:, SEQ - 1:SEQ])
                dve.wait_ge(S_["act_freed"], freed(7, 5)[1])
                dve.tensor_tensor(mixed[:, H + f, :], mixed[:, H + f, :], tt[:], ALU.mult).then_inc(
                    S_["lru_set"], 1)

            def k_norm(u, j):
                half = UNITS[u][1]
                n = tile_rows(j)
                g, n9 = FIRST_GROUP[u] + j, 9 * half + j
                dve.wait_ge(S_["k_pow"], n9 + 1)
                dve.wait_ge(S_["k_ss"], 2 * n9 + 2)
                if n9 >= 2:
                    dve.wait_ge(S_["kT_done"], n9 - 1)
                if n9 == 9:
                    dve.wait_ge(S_["stored_kv"], 16 * (2 + 2 * DB))
                dve.scalar_tensor_tensor(out=kn[0:n, n9 % 2, :], in0=pb[g % 3][0:n, 0:DH],
                                         scalar=stat[0:n, 16 + n9 % 2:17 + n9 % 2], in1=gain[0:n, 1, :],
                                         op0=ALU.mult, op1=ALU.mult).then_inc(S_["kn_set"], 1)

            def q_norm(u, j):
                half = UNITS[u][1]
                n = tile_rows(j)
                g, n9 = FIRST_GROUP[u] + j, 9 * half + j
                dve.wait_ge(S_["q_pow"], n9 + 1)
                if n9 >= 2:
                    dve.wait_ge(S_["qT_done"], n9 - 1)
                for i in range(2):
                    c = 24 + 2 * (n9 % 2) + i
                    ins = dve.scalar_tensor_tensor(out=qn[0:n, n9 % 2, i * DH:(i + 1) * DH],
                                                   in0=pb[g % 3][0:n, i * DH:(i + 1) * DH],
                                                   scalar=stat[0:n, c:c + 1], in1=gain[0:n, 0, :],
                                                   op0=ALU.mult, op1=ALU.mult)
                    ins.then_inc(S_["qn_set" if i else "qn_half"], 1)

            def wo_low(i):
                dve.wait_ge(S_["w_hi_set"], PIECES * NU + i + 1)
                dve.tensor_tensor(wo_part(i, 1), wo_raw[i % 4], wo_part(i, 0).bitcast(F32),
                                  ALU.subtract).then_inc(S_["w_lo_set"], 1)

            def m_low(t, piece):
                n, rows = tile_rows(t), M_ROWS[piece]
                dve.wait_ge(S_["m_hi_set"], m_count(t, piece))
                hi = m_hi[:, t % 2, rows, :] if t < NT else m_samp[:, rows, 0:NS]
                lo = m_lo[:, t % 2, rows, :] if t < NT else m_samp[:, rows, NS:]
                dve.tensor_tensor(lo, mixed[:, rows, chunk_cols(t)], hi.bitcast(F32), ALU.subtract).then_inc(
                                      S_["m_lo_set"], 1)

            def att_max(half, t):
                n8 = 8 * half + t
                lo = P if t == 0 else 0
                c = 32 + 8 * (n8 % 2)
                dve.wait_ge(S_["sc_done"], n8 + 1)
                if n8 == 0:
                    dve.wait_ge(S_["cc_in"], 16)
                if n8 >= 2:
                    dve.wait_ge(S_["pT_done"], n8 - 1)
                bias = cc[:, C_BIAS + half * 512:C_BIAS + (half + 1) * 512].rearrange("p (g n) -> p g n", g=2)
                ins = dve.scalar_tensor_tensor(out=pr[:, n8 % 2, :, lo:],
                                               in0=bb[1][:, :].rearrange("p (g n) -> p g n", g=2)[:, :, lo:],
                                               scalar=SCALE, in1=bias[:, :, lo:], op0=ALU.mult, op1=ALU.add)
                ins.then_inc(S_["biased"], 1)
                dve.wait_ge(S_["biased"], n8 + 1)
                sink = par[:, PAR["sink"] + 2 * half:PAR["sink"] + 2 * half + 2]
                link(dve.tensor_reduce(stat[:, c:c + 2], pr[:, n8 % 2, :, lo:], AX.X, ALU.max))
                link(dve.tensor_tensor(stat[:, c:c + 2], stat[:, c:c + 2], sink, ALU.max))
                link(dve.tensor_scalar(stat[:, c:c + 2], stat[:, c:c + 2], -1.0, None, ALU.mult))
                dve.tensor_tensor(stat[:, c + 2:c + 4], stat[:, c:c + 2], sink, ALU.add).then_inc(
                    S_["mx_set"], 1)

            def att_probs(half, t):
                n8 = 8 * half + t
                lo = P if t == 0 else 0
                c = 32 + 8 * (n8 % 2)
                dve.wait_ge(S_["ex_set"], 3 * n8 + 3)
                link(dve.tensor_tensor(stat[:, c + 4:c + 6], stat[:, c + 4:c + 6], stat[:, c + 2:c + 4], ALU.add))
                link(dve.reciprocal(stat[:, c + 4:c + 6], stat[:, c + 4:c + 6]))
                for g in range(2):
                    ins = dve.tensor_scalar(pr[:, n8 % 2, g, lo:], pr[:, n8 % 2, g, lo:],
                                            stat[:, c + 4 + g:c + 5 + g], None, ALU.mult)
                ins.then_inc(S_["pr_set"], 1)

            def att_mix(half, t):
                n8 = 8 * half + t
                dve.wait_ge(S_["av_done"], n8 + 1)
                m = mixed[:, 2 * H + 2 * half:2 * H + 2 * half + 2, chunk_cols(t)]
                dve.tensor_tensor(m, bb[3][:, 0:2 * P].rearrange("p (g n) -> p g n", g=2), m,
                                  ALU.mult).then_inc(S_["mix_c"], 1)

            def samp_max(half):
                dve.wait_ge(S_["ss_done"], half + 1)
                sc = kcT[0:64, 5:7, :].rearrange("p a n -> p (a n)")[:, 0:AKEYS]
                bias = cc[0:64, C_BIASS + half * AKEYS:C_BIASS + (half + 1) * AKEYS]
                sink = par[0:64, PAR["sink_s"] + half:PAR["sink_s"] + half + 1]
                link(dve.scalar_tensor_tensor(out=sc, in0=bb[4][0:64, 0:AKEYS], scalar=SCALE, in1=bias,
                                              op0=ALU.mult, op1=ALU.add))
                link(dve.tensor_reduce(stat[0:64, 48:49], sc, AX.X, ALU.max))
                link(dve.tensor_tensor(stat[0:64, 48:49], stat[0:64, 48:49], sink, ALU.max))
                link(dve.tensor_scalar(stat[0:64, 48:49], stat[0:64, 48:49], -1.0, None, ALU.mult))
                dve.tensor_tensor(stat[0:64, 49:50], stat[0:64, 48:49], sink, ALU.add).then_inc(S_["smx_set"], 1)

            def samp_probs(half):
                dve.wait_ge(S_["sex_set"], 2 * half + 2)
                link(dve.tensor_tensor(stat[0:64, 50:51], stat[0:64, 50:51], stat[0:64, 49:50], ALU.add))
                link(dve.reciprocal(stat[0:64, 50:51], stat[0:64, 50:51]))
                p = kcT[0:64, 2:4, :].rearrange("p a n -> p (a n)")[:, 0:AKEYS]
                dve.tensor_scalar(p, p, stat[0:64, 50:51], None, ALU.mult).then_inc(S_["spr_set"], 1)

            def samp_mix(half):
                dve.wait_ge(S_["sav_done"], half + 1)
                for g in range(2):
                    m = mixed[:, 2 * H + 2 * half + g, SEQ:TOK].rearrange("p (b i) -> p b i", b=DB)
                    o = bb[4][:, 0:64].rearrange("p (b g i) -> p b g i", b=DB, g=2)[:, :, g, :]
                    ins = dve.tensor_tensor(m, o, m, ALU.mult)
                    ins.then_inc(S_["smix_c" if g else "smix_half"], 1)

            def att_side(half, s):
                if s % 2 == 0 and 0 <= (s - 6) // 2 < NT:
                    att_probs(half, (s - 6) // 2)
                if s % 2 == 0 and 0 <= (s - 4) // 2 < NT:
                    att_max(half, (s - 4) // 2)
                if s % 2 == 0 and 0 <= (s - 12) // 2 < NT:
                    att_mix(half, (s - 12) // 2)
                if s == 25:
                    samp_max(half)
                if s == 27:
                    samp_probs(half)
                if s == 31:
                    samp_mix(half)

            def side(u, s):
                if s - 1 in W_AT and u + 1 < NU:
                    w_low(u + 1, W_AT.index(s - 1))
                if u in RET_UNIT and s < 12:
                    base = 9 * RET_UNIT[u]
                    if s < 9:
                        ret_mask(base + s)
                    if 1 <= s < 10:
                        ret_state(base + s - 1)
                    if s >= 3:
                        ret_mix(base + s - 3)
                if u == 1 and s == 3:
                    dve.wait_ge(S_["st_turned"], 1)
                    dve.tensor_copy(st_T[:].rearrange("p f n -> p (f n)"), bb[4][:, 0:H * NS]).then_inc(
                        S_["st_copied"], 1)
                if (u, s) == (1, 6):
                    softplus()
                if (u, s) in ((17, 7), (17, 9)):
                    wo_low((s - 7) // 2)
                if (u, s) in ((17, 4), (17, 5)):
                    m_low(s - 4, 0)
                if (u, s) == (17, 10):
                    m_low(0, 1)
                    m_low(1, 1)
                if (u, s) in LRU_AT["conv"]:
                    conv(LRU_AT["conv"][u, s])
                if (u, s) in LRU_AT["m2"]:
                    lru_m2(LRU_AT["m2"][u, s])
                if (u, s) in LRU_AT["scan"]:
                    lru_scan(LRU_AT["scan"][u, s])
                if att_slot(u, s):
                    att_side(*att_slot(u, s))

            for u in range(NU):
                if u == 0:
                    x_scale(0)
                    x_scale(1)
                    x_lo(0)
                    for i in range(PIECES):
                        w_low(0, i)
                    x_scale(2)
                    x_lo(1)
                for j in range(n_groups(u)):
                    if u == 0:
                        if j + 3 <= NT:
                            x_scale(j + 3)
                        if j + 2 <= NT:
                            x_lo(j + 2)
                    side(u, 2 * j)
                    if j == NT:
                        bank = pb[(FIRST_GROUP[u] + j) % 3]
                        dve.wait_ge(S_["fold_set"], FOLDS.index(u) + 1)
                        dve.tensor_tensor(bank[0:NS, 0:UNIT], bank[0:NS, 0:UNIT], junk[0:NS, :],
                                          ALU.add).then_inc(S_["folded"], 1)
                    if UNITS[u][0] == "kvC":
                        k_norm(u, j)
                    if UNITS[u][0] == "qC":
                        q_norm(u, j)
                    if UNITS[u][0] == "gA":
                        e = 6 * UNITS[u][1] + j
                        dve.wait_ge(S_["act_freed"], freed(u, j)[1])
                        row, cols = e // 3, slice((e % 3) * CH, (e % 3 + 1) * CH)
                        dve.tensor_tensor(mixed[:, row, cols], mixed[:, row, cols], gate_tmp[:, e % 2, :],
                                          ALU.mult).then_inc(S_["mix_g"], 1)
                    side(u, 2 * j + 1)

            for i in range(2, KM):
                wo_low(i)
            for t in range(NT + 1):
                n = tile_rows(t)
                for piece in range(2):
                    if t + 2 <= NT:
                        m_low(t + 2, piece)
                dve.wait_ge(S_[f"x_again{t % 2}"], 16 * (t // 2 + 1))
                if t >= 2:
                    dve.wait_ge(S_[f"stored_y{t % 2}"], 16 * (t // 2))
                if t == NT:
                    dve.wait_ge(S_["ys_done"], 2)
                    for q in range(2):
                        cols = slice(q * 512, (q + 1) * 512)
                        link(dve.tensor_tensor(x_res[0:n, t % 2, cols], y_banks[t % 3][q][0:n, :],
                                               x_res[0:n, t % 2, cols], ALU.add))
                        dve.wait_ge(S_["ys_copied"], q + 1)
                        link(dve.tensor_tensor(x_res[0:n, t % 2, cols], y_out[0:n, 1, cols],
                                               x_res[0:n, t % 2, cols], ALU.add))
                banks = ys_banks if t == NT else y_banks[t % 3]
                for q in range(2):
                    cols = slice(q * 512, (q + 1) * 512)
                    dve.wait_ge(S_["y_done"], 2 * t + q + 1)
                    dve.tensor_tensor(y_out[0:n, t % 2, cols], banks[q][0:n, :],
                                      x_res[0:n, t % 2, cols], ALU.add).then_inc(S_["y_set"], 1)

        @block.gpsimd
        def _(pool):
            count = [0]

            def link(ins):
                count[0] += 1
                ins.then_inc(S_["chain_p"], 1)
                pool.wait_ge(S_["chain_p"], count[0])

            def root(ss, rs, n, width):
                w = ss.shape[1]
                link(pool.tensor_scalar(ss, ss, 1.0 / width, EPS, ALU.mult, ALU.add))
                return pool.tensor_tensor(rs, ss, neghalf[0:n, 0:w], ALU.pow)

            def ret_qdec(m):
                hd, c = divmod(m, 9)
                n = tile_rows(c)
                if m == 0:
                    pool.wait_ge(S_["cr_in"], 16)
                if c == 0:
                    pool.wait_ge(S_["act_freed"], freed(UNITS.index(("qk", hd)), 5)[1])
                if m >= 2:
                    pool.wait_ge(S_["o_done"], m - 1)
                dec = cr[:, C_QDEC + hd * P:C_QDEC + (hd + 1) * P] if c < NT else \
                    cr[:, C_QDECS + hd * NS:C_QDECS + (hd + 1) * NS]
                pool.tensor_tensor(q_dec[:, m % 2, 0:n], qk[hd][:, 0, chunk_cols(c)], dec, ALU.mult).then_inc(
                    S_["qdec_set"], 1)
                if c < DB:
                    if c == 0:
                        pool.wait_ge(S_["act_freed"], freed(UNITS.index(("v", hd // 2)), 8)[1])
                        if hd > 0:
                            pool.wait_ge(S_["kv2_done"], hd)
                    col = C_VSEL + hd * DB + c
                    pool.tensor_scalar(v_sel[:, c, :], v_tok[0:NS, hd // 2, NT, (hd % 2) * DH:(hd % 2 + 1) * DH],
                                       cr[0:NS, col:col + 1], None, ALU.mult).then_inc(S_["vsel_set"], 1)

            def ret_root(m):
                hd, c = divmod(m, 9)
                pool.wait_ge(S_["o_ss"], m + 1)
                root(stat[:, 4 + m % 2:5 + m % 2], stat[:, 8 + m % 2:9 + m % 2], P, DH).then_inc(S_["o_pow"], 1)

            link(pool.memset(neghalf[:], -0.5))
            pool.memset(ones[:], 1.0).then_inc(S_["ones_set"], 1)
            for t in range(NT + 1):
                n = tile_rows(t)
                pool.wait_ge(S_["x_ss"], t + 1)
                root(stat[0:n, t % XS:t % XS + 1], stat[0:n, 52 + t % XS:53 + t % XS], n, D).then_inc(S_["x_pow"], 1)
            for hd in range(H):
                for c in range(NT + 1):
                    ret_qdec(9 * hd + c)
                    if c >= 1:
                        ret_root(9 * hd + c - 1)
            for half in range(2):
                for j in range(NT + 1):
                    n, n9 = tile_rows(j), 9 * half + j
                    pool.wait_ge(S_["k_ss"], 2 * n9 + 1)
                    root(stat[0:n, 12 + n9 % 2:13 + n9 % 2], stat[0:n, 16 + n9 % 2:17 + n9 % 2], n, DH).then_inc(
                        S_["k_pow"], 1)
                for j in range(NT + 1):
                    n, n9 = tile_rows(j), 9 * half + j
                    c = 2 * (n9 % 2)
                    pool.wait_ge(S_["q_ss"], 2 * n9 + 2)
                    root(stat[0:n, 20 + c:22 + c], stat[0:n, 24 + c:26 + c], n, DH).then_inc(S_["q_pow"], 1)


def constants():
    log_g = np.log1p(-np.power(2.0, -5.0 - np.arange(H)))
    i = np.arange(P)
    d = i[None, :] - i[:, None]
    cr = np.zeros((P, N_CR))
    for h in range(H):
        cr[:, C_MASK + h * P:C_MASK + (h + 1) * P] = np.where(d >= 0, np.exp(np.maximum(d, 0) * log_g[h]), 0) * SCALE
        cr[:, C_QDEC + h * P:C_QDEC + (h + 1) * P] = np.exp((i + 1) * log_g[h])[None, :]
        cr[:, C_KDEC + h] = np.exp((P - 1 - i) * log_g[h]) * SCALE
        t = np.arange(NS)
        same = (t[:, None] // DS) == (t[None, :] // DS)
        ds = t[None, :] - t[:, None]
        cr[:NS, C_MASKS + h * NS:C_MASKS + (h + 1) * NS] = \
            np.where(same & (ds >= 0), np.exp(np.maximum(ds, 0) * log_g[h]), 0) * SCALE
        cr[:, C_QDECS + h * NS:C_QDECS + (h + 1) * NS] = np.exp((t % DS + 1) * log_g[h])[None, :]
        for b in range(DB):
            cr[:NS, C_VSEL + h * DB + b] = (t // DS == b) * np.exp((DS - 1 - t % DS) * log_g[h]) * SCALE
    slope = 2.0 ** (-8.0 * np.arange(1, H + 1) / H)
    cc = np.zeros((P, N_CC))
    k = np.arange(2 * P) - P
    dist = i[:, None] - k[None, :]
    for h in range(H):
        cc[:, C_BIAS + h * 2 * P:C_BIAS + (h + 1) * 2 * P] = \
            np.where((dist >= 0) & (dist < WINDOW), -slope[h] * dist, NEG)
    rows = [(b, g, s) for b in range(DB) for g in range(2) for s in range(DS)]
    for half in range(2):
        for r, (b, g, s) in enumerate(rows):
            dist = s + WINDOW - np.arange(WINDOW)
            row = np.full(AKEYS, NEG)
            row[:WINDOW] = np.where(dist < WINDOW, -slope[2 * half + g] * dist, NEG)
            for j in range(s + 1):
                row[WINDOW + b * DS + j] = -slope[2 * half + g] * (s - j)
            cc[r, C_BIASS + half * AKEYS:C_BIASS + (half + 1) * AKEYS] = row
    return {"c_ident": np.eye(P, dtype=np.float32), "c_ret": cr.astype(np.float32), "c_att": cc.astype(np.float32)}


def laid_out(x):
    f = {k: np.asarray(v) for k, v in x.items()}
    base = {"qk0": 0, "v": 1024, "gA": 1536, "xb": 2048, "gB": 2560, "qC": 3072, "kC": 3584, "vC": 3840, "gC": 4096}
    w = f["w_in"][0]
    units = []
    for kind, i in UNITS:
        if kind == "qk":
            cols = [w[:, i * DH:(i + 1) * DH], w[:, GW + i * DH:GW + (i + 1) * DH]]
        elif kind == "kvC":
            cols = [w[:, base[n] + i * DH:base[n] + (i + 1) * DH] for n in ("kC", "vC")]
        else:
            cols = [w[:, base[kind] + i * UNIT:base[kind] + (i + 1) * UNIT]]
        unit = np.concatenate(cols, axis=1)
        units.append(unit.reshape(KD, P, UNIT).transpose(1, 0, 2).reshape(P, KD * UNIT))
    par = np.zeros((P, N_PAR), np.float32)

    def put(name, rows):
        par[:, PAR[name]:PAR[name] + rows.shape[0]] = rows.T

    put("ret_g", f["ret_norm_g"].reshape(H, P))
    put("conv_w", f["conv_w"].reshape(CONV * H, P))
    put("conv_b", f["conv_b"].reshape(H, P))
    put("b_r", f["b_rgate"].reshape(H, P))
    put("b_i", f["b_igate"].reshape(H, P))
    put("lam", f["lru_lambda"].reshape(H, P))
    par[:, PAR["sink"]:PAR["sink"] + H] = f["attn_sinks"]
    for half in range(2):
        for r in range(2 * NS):
            par[r, PAR["sink_s"] + half] = f["attn_sinks"][0, 2 * half + r // DS % 2]
    wg = np.zeros((P, 2, H, P), np.float32)
    for a, name in enumerate(("w_rgate", "w_igate")):
        blocks = f[name][0]
        for n in range(2 * H):
            r = slice(64 * (n % 2), 64 * (n % 2) + 64)
            wg[r, a, n // 2, r] = blocks[n]
    return {
        "x_prompt": f["x_prompt"].reshape(SEQ, D), "x_sample": f["x_sample"].reshape(NS, D),
        "w_units": np.stack(units), "w_out": f["w_out"][0], "norm_g": f["norm_g"].reshape(D), "params": par,
        "qk_gain": np.concatenate([f["q_norm_g"][0], f["k_norm_g"][0]]),
        "w_gates": wg.reshape(P, 2 * H * P), "state_conv": f["state_conv"].reshape(DB * 3, GW),
        "state_lru": f["state_lru"].reshape(DB, GW), "state_ret": f["state_ret"][0],
        "cache_k": f["cache_swa_k"][0], "cache_v": f["cache_swa_v"][0], **constants(),
    }


OUTS = {"y_prompt": (SEQ, D), "y_sample": (NS, D), "p_ret": (H, DH, DH), "p_lru": (1, GW), "p_conv": (3, GW),
        "p_k": (WINDOW, 2, DH), "p_v": (WINDOW, 2, DH), "s_ret": (DB, H, DH, DH), "s_lru": (DB, GW),
        "s_conv": (DB * 3, GW), "s_k": (DB, WINDOW, 2, DH), "s_v": (DB, WINDOW, 2, DH)}
SHAPES = [(1, SEQ, D), (DB, DS, D), (1, 1, H, DH, DH), (1, 1, GW), (1, 1, 3, GW), (1, 1, WINDOW, 2, DH),
          (1, 1, WINDOW, 2, DH), (1, DB, H, DH, DH), (1, DB, GW), (1, DB, 3, GW), (1, DB, WINDOW, 2, DH),
          (1, DB, WINDOW, 2, DH)]


def kernel(**inputs):
    import concourse.bacc as bacc
    from concourse.bass_utils import run_bass_kernel_spmd

    nc = bacc.Bacc("TRN2", target_bir_lowering=False, num_devices=1)
    arrays = {k: np.ascontiguousarray(v) for k, v in laid_out(inputs).items()}
    io = {k: nc.dram_tensor(k, v.shape, F32, kind="ExternalInput").ap() for k, v in arrays.items()}
    for name, shape in OUTS.items():
        io[name] = nc.dram_tensor(f"out_{name}", shape, F32, kind="ExternalOutput").ap()
    layer(nc, io)
    r = run_bass_kernel_spmd(nc, [arrays], core_ids=[0]).results[0]
    return tuple(r[f"out_{name}"].reshape(shape) for name, shape in zip(OUTS, SHAPES))
```
